# Optimizing a Trainium2 kernel written in Bass

```python
import jax, jax.numpy as jnp
from jax import lax
import numpy as np

D_MODEL = 1024
BATCH = 1
SEQ = 256
DEPTH = 2

GRID_W = 64
RMS_EPS = 1e-6
LB_FLOOR = 1e-12
MASK_VALUE = -1e30
A_DK = 128
A_DV = A_DK
A_WIDTH = D_MODEL // 2
A_HEADS = A_WIDTH // A_DK
HGRN_CHUNK = 32
B_DH = 64
B_WIDTH = D_MODEL - A_WIDTH
B_HEADS = B_WIDTH // B_DH
NA_KR = 8
NA_KC = 16
C_CONFIGS = ((128, 1), (512, 4), (2048, 16))
C_GROUPS = len(C_CONFIGS)
C_DH = 64
C_WIDTH = D_MODEL // 2
C_HPG = C_WIDTH // C_DH
ATTN_BLOCK = 128
POOL_WINDOWS = (2, 4, 8, 16)
POOL_CH = D_MODEL - C_WIDTH
POOL_GC = POOL_CH // len(POOL_WINDOWS)
D_FF = ((8 * D_MODEL // 3 + 255) // 256) * 256
FFN_CONV = 3
EVEN_IN = 5 * A_WIDTH + 3 * B_WIDTH
ODD_IN = 3 * C_GROUPS * C_WIDTH + POOL_CH
MIX_W = D_MODEL
N_EVEN = (DEPTH + 1) // 2
N_ODD = DEPTH // 2

kernel_name = 'hybrid_hgrn2_natten_dilated_pool_encoder'

F32 = jnp.float32

def _rmsnorm(x, g):
    xf = x.astype(F32)
    y = xf * lax.rsqrt(jnp.mean(xf * xf, axis=-1, keepdims=True) + RMS_EPS)
    return (y * g.astype(F32)).astype(x.dtype)

def _alibi_slopes(n):
    return jnp.exp2(-8.0 * jnp.arange(1, n + 1, dtype=F32) / n)

def _gla_scan(q, k, v, log_f):
    B, H, T, DK = q.shape
    DV = v.shape[-1]
    n = T // HGRN_CHUNK

    def chunks(a):
        return jnp.moveaxis(a.reshape(B, H, n, HGRN_CHUNK, a.shape[-1]), 2, 0)

    tril = jnp.tril(jnp.ones((HGRN_CHUNK, HGRN_CHUNK), dtype=bool))[:, :, None]

    def step(S, inp):
        qc, kc, vc, lfc = inp
        b = jnp.cumsum(lfc, axis=2)
        b_last = b[:, :, -1:, :]
        diff = b[:, :, :, None, :] - b[:, :, None, :, :]
        decay = jnp.where(tril, jnp.exp(jnp.where(tril, diff, 0.0)), 0.0)
        att = jnp.einsum('bhck,bhsk,bhcsk->bhcs', qc, kc, decay)
        o = jnp.einsum('bhcs,bhsv->bhcv', att, vc) + jnp.einsum('bhck,bhkv->bhcv', qc * jnp.exp(b), S)
        S = jnp.exp(b_last[:, :, 0, :, None]) * S + jnp.einsum('bhsk,bhsv->bhkv', kc * jnp.exp(b_last - b), vc)
        return S, o

    S0 = jnp.zeros((B, H, DK, DV), F32)
    _, o = lax.scan(step, S0, (chunks(q), chunks(k), chunks(v), chunks(log_f)))
    return jnp.moveaxis(o, 0, 2).reshape(B, H, T, DV)

def _hgrn2(z, lb, norm_g):
    B, T, _ = z.shape
    q, f_fwd, f_bwd, i, g = jnp.split(z.astype(F32), 5, axis=-1)

    def heads(a):
        return a.reshape(B, T, A_HEADS, -1).transpose(0, 2, 1, 3)

    q = heads(jax.nn.silu(q))
    v = heads(i)
    lb = lb.astype(F32).reshape(A_HEADS, 1, A_DK)
    log_lb = jnp.log(jnp.maximum(lb, LB_FLOOR))
    log_1m_lb = jnp.log1p(-lb)

    def gates(fz):
        fz = heads(fz)
        log_f = jnp.logaddexp(log_lb, log_1m_lb + jax.nn.log_sigmoid(fz))
        k = (1.0 - lb) * jax.nn.sigmoid(-fz)
        return k, log_f

    k_f, lf_f = gates(f_fwd)
    k_b, lf_b = gates(f_bwd)
    o_fwd = _gla_scan(q, k_f, v, lf_f)
    flip = lambda a: jnp.flip(a, axis=2)
    o_bwd = flip(_gla_scan(flip(q), flip(k_b), flip(v), flip(lf_b)))
    o = o_fwd + o_bwd
    o = o * lax.rsqrt(jnp.mean(o * o, axis=-1, keepdims=True) + RMS_EPS) * norm_g.astype(F32)
    return o.transpose(0, 2, 1, 3).reshape(B, T, A_WIDTH) * jax.nn.silu(g)

def _neighbourhood_attention(q, k, v, rpb):
    B, T, H, DH = q.shape
    rows = T // GRID_W
    kr = min(NA_KR, rows)
    grid = lambda a: a.astype(F32).reshape(B, rows, GRID_W, H, DH)
    qg, kg, vg = grid(q), grid(k), grid(v)
    col = jnp.arange(GRID_W)
    col_idx = jnp.clip(col - NA_KC // 2, 0, GRID_W - NA_KC)[:, None] + jnp.arange(NA_KC)[None, :]
    rpb_col = rpb.astype(F32)[:, :, col_idx - col[:, None] + NA_KC - 1]
    scale = DH ** -0.5

    def row_block(args):
        r, q_row = args
        rs = jnp.clip(r - kr // 2, 0, rows - kr)
        k_win = lax.dynamic_slice_in_dim(kg, rs, kr, axis=1)[:, :, col_idx]
        v_win = lax.dynamic_slice_in_dim(vg, rs, kr, axis=1)[:, :, col_idx]
        bias = rpb_col[:, rs + jnp.arange(kr) - r + NA_KR - 1]
        s = jnp.einsum('bchd,bicjhd->bhcij', q_row, k_win) * scale + jnp.transpose(bias, (0, 2, 1, 3))[None]
        p = jax.nn.softmax(s.reshape(B, H, GRID_W, kr * NA_KC), axis=-1).reshape(s.shape)
        return jnp.einsum('bhcij,bicjhd->bchd', p, v_win)

    o = lax.map(row_block, (jnp.arange(rows), jnp.moveaxis(qg, 1, 0)))
    return jnp.moveaxis(o, 0, 1).reshape(B, T, H * DH)

def _dilated_attention(q, k, v, slopes):
    B, T = q.shape[:2]
    scale = C_DH ** -0.5

    def block(t0):
        pos = t0 + jnp.arange(ATTN_BLOCK)
        q_blk = lax.dynamic_slice_in_dim(q, t0, ATTN_BLOCK, axis=1).astype(F32)
        outs, lses = [], []
        for g, (window, dil) in enumerate(C_CONFIGS):
            per_side = window // 2 // dil
            offs = dil * jnp.arange(-per_side, per_side + 1)
            idx = pos[:, None] + offs[None, :]
            valid = (idx >= 0) & (idx < T)
            idx = jnp.clip(idx, 0, T - 1)
            k_sel = k[:, idx, g].astype(F32)
            v_sel = v[:, idx, g].astype(F32)
            s = jnp.einsum('bqhd,bqjhd->bhqj', q_blk[:, :, g], k_sel) * scale
            s = s - slopes[g][:, None, None] * jnp.abs(offs).astype(F32)
            s = jnp.where(valid, s, MASK_VALUE)
            m = jnp.max(s, axis=-1, keepdims=True)
            p = jnp.exp(s - m)
            den = jnp.sum(p, axis=-1, keepdims=True)
            outs.append(jnp.einsum('bhqj,bqjhd->bhqd', p / den, v_sel))
            lses.append(m + jnp.log(den))
        w = jax.nn.softmax(jnp.stack(lses), axis=0)
        o = jnp.sum(w * jnp.stack(outs), axis=0)
        return jnp.transpose(o, (0, 2, 1, 3))

    o = lax.map(block, jnp.arange(T // ATTN_BLOCK) * ATTN_BLOCK)
    return jnp.moveaxis(o, 0, 1).reshape(B, T, C_HPG * C_DH)

def _multiscale_pool(u, w_groups, scale):
    B, T, _ = u.shape
    uf = u.astype(F32)
    cs = jnp.concatenate([jnp.zeros((B, 1, POOL_CH), F32), jnp.cumsum(uf, axis=1)], axis=1)
    t = jnp.arange(T)
    outs = []
    for g, w in enumerate(POOL_WINDOWS):
        lo = jnp.clip(t - w // 2, 0, T)
        hi = jnp.clip(t + w - w // 2, 0, T)
        sl = slice(g * POOL_GC, (g + 1) * POOL_GC)
        mean = (cs[:, hi, sl] - cs[:, lo, sl]) / (hi - lo).astype(F32)[None, :, None]
        outs.append(jnp.einsum('btc,cd->btd', mean - uf[:, :, sl], w_groups[g].astype(F32)))
    return (jnp.concatenate(outs, axis=-1) * scale.astype(F32)).astype(u.dtype)

def _conv_ffn(h, w_up, conv_w, conv_b, w_down):
    T = h.shape[1]
    gate, val = jnp.split(h @ w_up, 2, axis=-1)
    gp = jnp.pad(gate, ((0, 0), (FFN_CONV // 2, FFN_CONV // 2), (0, 0)))
    gate = conv_b + sum(gp[:, j:j + T] * conv_w[j] for j in range(FFN_CONV))
    return (jax.nn.silu(gate) * val) @ w_down

def setup_inputs(seed: int = 0) -> dict:
    key = jax.random.key(seed)
    ks = jax.random.split(key, 20)
    nrm = lambda k, shape, s=1.0: s * jax.random.normal(k, shape, F32)
    return {
        'x': nrm(ks[0], (BATCH, SEQ, D_MODEL)),
        'c': nrm(ks[1], (BATCH, D_MODEL)),
        'ada_w': nrm(ks[2], (DEPTH, D_MODEL, 6 * D_MODEL), 0.5 * D_MODEL ** -0.5),
        'ada_b': nrm(ks[3], (DEPTH, 6 * D_MODEL), 0.02),
        'norm_mix_g': 1.0 + nrm(ks[4], (DEPTH, D_MODEL), 0.1),
        'norm_ffn_g': 1.0 + nrm(ks[5], (DEPTH, D_MODEL), 0.1),
        'even_w_in': nrm(ks[6], (N_EVEN, D_MODEL, EVEN_IN), D_MODEL ** -0.5),
        'even_w_out': nrm(ks[7], (N_EVEN, MIX_W, D_MODEL), MIX_W ** -0.5),
        'hgrn_lb_logits': nrm(ks[8], (N_EVEN, A_WIDTH)),
        'hgrn_norm_g': 1.0 + nrm(ks[9], (N_EVEN, A_DV), 0.1),
        'na_rpb': nrm(ks[10], (N_EVEN, B_HEADS, 2 * NA_KR - 1, 2 * NA_KC - 1), 0.1),
        'odd_w_in': nrm(ks[11], (N_ODD, D_MODEL, ODD_IN), D_MODEL ** -0.5),
        'odd_w_out': nrm(ks[12], (N_ODD, MIX_W, D_MODEL), MIX_W ** -0.5),
        'pool_w': nrm(ks[13], (N_ODD, len(POOL_WINDOWS), POOL_GC, POOL_GC), POOL_GC ** -0.5),
        'pool_scale': 1.0 + nrm(ks[14], (N_ODD, POOL_CH), 0.1),
        'ffn_w_up': nrm(ks[15], (DEPTH, D_MODEL, 2 * D_FF), D_MODEL ** -0.5),
        'ffn_conv_w': nrm(ks[16], (DEPTH, FFN_CONV, D_FF), FFN_CONV ** -0.5),
        'ffn_conv_b': nrm(ks[17], (DEPTH, D_FF), 0.02),
        'ffn_w_down': nrm(ks[18], (DEPTH, D_FF, D_MODEL), D_FF ** -0.5),
        'final_norm_g': 1.0 + nrm(ks[19], (D_MODEL,), 0.1),
    }

def reference(x, c, ada_w, ada_b, norm_mix_g, norm_ffn_g, even_w_in, even_w_out, hgrn_lb_logits, hgrn_norm_g, na_rpb, odd_w_in, odd_w_out, pool_w, pool_scale, ffn_w_up, ffn_conv_w, ffn_conv_b, ffn_w_down, final_norm_g):
    B, T, _ = x.shape
    lb_soft = jax.nn.softmax(hgrn_lb_logits.astype(F32), axis=0)
    lower_bounds = jnp.cumsum(lb_soft, axis=0) - lb_soft[0]
    slopes = _alibi_slopes(C_GROUPS * C_HPG).reshape(C_GROUPS, C_HPG)
    c_act = jax.nn.silu(c)
    n_c = 3 * C_GROUPS * C_WIDTH
    for l in range(DEPTH):
        mod = c_act @ ada_w[l] + ada_b[l]
        sh1, sc1, g1, sh2, sc2, g2 = jnp.split(mod[:, None, :], 6, axis=-1)
        h = _rmsnorm(x, norm_mix_g[l]) * (1.0 + sc1) + sh1
        if l % 2 == 0:
            e = l // 2
            z = h @ even_w_in[e]
            o_a = _hgrn2(z[..., :5 * A_WIDTH], lower_bounds[e], hgrn_norm_g[e])
            q_b, k_b, v_b = jnp.split(z[..., 5 * A_WIDTH:], 3, axis=-1)
            shape_b = (B, T, B_HEADS, B_DH)
            o_b = _neighbourhood_attention(q_b.reshape(shape_b), k_b.reshape(shape_b), v_b.reshape(shape_b), na_rpb[e])
            mixed = jnp.concatenate([o_a.astype(h.dtype), o_b.astype(h.dtype)], axis=-1) @ even_w_out[e]
        else:
            o_i = l // 2
            z = h @ odd_w_in[o_i]
            q_c, k_c, v_c = jnp.split(z[..., :n_c], 3, axis=-1)
            shape_c = (B, T, C_GROUPS, C_HPG, C_DH)
            o_c = _dilated_attention(q_c.reshape(shape_c), k_c.reshape(shape_c), v_c.reshape(shape_c), slopes)
            o_d = _multiscale_pool(z[..., n_c:], pool_w[o_i], pool_scale[o_i])
            mixed = jnp.concatenate([o_c.astype(h.dtype), o_d], axis=-1) @ odd_w_out[o_i]
        x = x + g1 * mixed
        h = _rmsnorm(x, norm_ffn_g[l]) * (1.0 + sc2) + sh2
        x = x + g2 * _conv_ffn(h, ffn_w_up[l], ffn_conv_w[l], ffn_conv_b[l], ffn_w_down[l])
    return _rmsnorm(x, final_norm_g)


_drawn_inputs = setup_inputs


def setup_inputs(seed=0):
    import zlib

    import numpy as np

    out = dict(_drawn_inputs(seed))
    spreads = {}
    factors = {'hgrn_norm_g': 3.635, 'na_rpb': 8.0, 'pool_scale': 3.041, 'ffn_conv_b': 8.0}
    for name, (base, spread) in spreads.items():
        noise = np.random.default_rng([zlib.crc32(name.encode()), seed]).standard_normal(out[name].shape)
        drawn = base * np.exp(spread * noise) if base else spread * noise
        out[name] = __import__('jax').numpy.asarray(drawn.astype(out[name].dtype))
    for name, factor in factors.items():
        out[name] = (out[name] * factor).astype(out[name].dtype)
    return out
```

```python
from contextlib import ExitStack

import numpy as np

import concourse.bass as bass
from concourse import mybir

ALU = mybir.AluOpType
ACT = mybir.ActivationFunctionType
AX_X = mybir.AxisListType.X
F32 = mybir.dt.float32
F32R = mybir.dt.float32r
I32 = mybir.dt.int32

P = 128
D = 1024
T = 256
KT = D // P
TT = T // P
EPS = 1e-6
LB_FLOOR = 1e-12
BIG = 1e30
D_FF = 2816
FT = D_FF // P
GRID_W, NA_KR, NA_KC = 64, 8, 16
NA_HEADS, DH = 8, 64
A_HEADS = 4
C_GROUPS, C_HEADS = 3, 8
C_CONFIGS = ((128, 1), (512, 4), (2048, 16))
WINDOWS = (2, 4, 8, 16)
SCALE = DH ** -0.5

UNIT = 2048
RAW = 4
SPLIT = 2
EI, EO, UP0, DN0, OI, OO, UP1, DN1, UNITS = (0, 16, 20, 42, 53, 73, 77, 99, 110)
N_EI, N_EO, N_UP, N_DN, N_OI, N_OO = 16, 4, FT, FT // 2, 20, 4
ADA0, ADA1, ADA2, ADA3, ADAS = 0, 8, 40, 56, 88

LEVELS = (1, 2, 4, 8, 16, 32, 64, 128)
GLA_STEPS = [(0, 0)] + [(d, h) for h in LEVELS for d in (0, 1)]
SMALL = [s for s, (_, h) in enumerate(GLA_STEPS) if h < 64]
SB = 64
STEPS = 16
RES = 4
ROW = T + 2 * T // RES

C_ID, C_MEAN, C_EPS = 0, 128, 256
C_PICK = C_EPS + 1
C_HMEAN = C_PICK + 63
C_DIST = C_HMEAN + P
C_SLOPE = C_DIST + TT * ROW
C_NAT = C_SLOPE + 2 * C_HEADS
C_LVL = C_NAT + GRID_W
C_INV = C_LVL + 12 * SB
C_FLIP = C_INV + 4 * T
C_ALL = C_FLIP + P

V_C, V_ADAB = 0, 8
V_NMIX, V_NFFN, V_FIN, V_PSC, V_LB, V_HG, V_CB = 104, 120, 136, 144, 148, 152, 153
V_CW = 197
V_ALL = V_CW + 2 * 3 * FT


NORM_AT = (0, 10, 18, 28)
MIX_AT = (8, 26)


def slope(g, h):
    return 2.0 ** (-8.0 * (g * C_HEADS + h + 1) / (C_GROUPS * C_HEADS))


def shape_constants():
    a = np.zeros((P, C_ALL), np.float32)
    p = np.arange(P)
    a[:, C_ID:C_ID + P] = np.eye(P)
    a[:, C_MEAN:C_MEAN + P] = 1.0 / D
    a[:, C_HMEAN:C_HMEAN + P] = 1.0 / P
    key = np.arange(T)
    half, b = p // 64, p % 64
    for t in range(TT):
        query = RES * b + 2 * t + half
        keys = np.concatenate([np.tile(RES * (key % 64) + key // 64, (P, 1)), np.tile(RES * np.arange(64), (P, 2)) + (2 * t + half)[:, None]], 1)
        group = np.concatenate([np.zeros((P, T), int), np.repeat(np.where(half, 2, 1)[:, None], 64, 1),
                                np.repeat(np.where(half, 1, 2)[:, None], 64, 1)], 1)
        off = np.abs(keys - query[:, None])
        window = np.array([w for w, _ in C_CONFIGS])[group]
        dil = np.array([d for _, d in C_CONFIGS])[group]
        ok = (off % dil == 0) & (off <= window // 2 // dil * dil)
        a[:, C_DIST + t * ROW:C_DIST + (t + 1) * ROW] = np.where(ok, off, BIG)
    for h in range(C_HEADS):
        a[:, C_SLOPE + 2 * h] = np.where(half, -slope(2, h), -slope(1, h))
        a[:, C_SLOPE + 2 * h + 1] = np.where(half, -slope(1, h), -slope(2, h))
    c, kc = (p % GRID_W)[:, None], np.arange(GRID_W)[None, :]
    first = np.clip(c - NA_KC // 2, 0, GRID_W - NA_KC)
    a[:, C_NAT:C_NAT + GRID_W] = np.where((kc >= first) & (kc < first + NA_KC), 0.0, -BIG)
    s, q = (p % SB)[:, None], np.arange(SB)[None, :]
    for d in (0, 1):
        for n, h in enumerate(LEVELS[:6]):
            same = s // (2 * h) == q // (2 * h)
            late, early = (q, s) if d == 0 else (s, q)
            at = C_LVL + (d * 6 + n) * SB
            a[:, at:at + SB] = same & (late % (2 * h) >= h) & (early % (2 * h) < h)
    for g, w in enumerate(WINDOWS):
        lo, hi = np.clip(key - w // 2, 0, T), np.clip(key + w - w // 2, 0, T)
        a[:, C_INV + g * T:C_INV + (g + 1) * T] = 1.0 / (hi - lo).astype(np.float32)
    a[:, C_EPS] = EPS
    a[:, C_PICK + 31] = 1.0
    a[:, C_FLIP:C_FLIP + P] = (p[:, None] // GRID_W == p[None, :] // GRID_W) & (p[:, None] % GRID_W + p[None, :] % GRID_W == GRID_W - 1)
    return a


def encoder(nc, x, c, ada_w, ada_b, norm_mix_g, norm_ffn_g, even_w_in, even_w_out, hgrn_lb_logits, hgrn_norm_g,
            na_rpb, odd_w_in, odd_w_out, pool_w, pool_scale, ffn_w_up, ffn_conv_w, ffn_conv_b, ffn_w_down,
            final_norm_g, consts_in, out):
    with ExitStack() as ctx:
        place = [(nc.sbuf_base + 63) // 64 * 64]

        def at(name, shape, dt, offset):
            return nc.alloc_sbuf_tensor_at(name, shape, dt, offset=offset)

        def sb(name, shape, dt=F32):
            n = 4
            for s in shape[1:]:
                n *= s
            t = at(name, shape, dt, place[0])
            place[0] += (n + 63) // 64 * 64
            return t

        def sem(name):
            return ctx.enter_context(nc.semaphore(name))

        w_raw = sb("w_raw", [P, RAW, UNIT])
        w_hi = sb("w_hi", [P, SPLIT, UNIT], F32R)
        w_lo = sb("w_lo", [P, SPLIT, UNIT], F32R)
        ada_raw = sb("ada_raw", [P, 2, 1024])
        mod_acc = sb("mod_acc", [P, 4096])
        xT = sb("xT", [P, KT, T])
        h_at = place[0]
        h_hi = sb("h_hi", [P, KT, T], F32R)
        h_lo = sb("h_lo", [P, KT, T], F32R)
        work = sb("work", [P, KT, T])
        consts = sb("consts", [P, C_ALL])
        vecs = sb("vecs", [P, V_ALL])
        cact = sb("cact", [P, KT])
        mods = sb("mods", [P, 2, 48])
        gain = sb("gain", [P, 4, KT])
        rstd = sb("rstd", [P, T])
        lbt = sb("lbt", [P, 6, A_HEADS])
        mod_rows = sb("mod_rows", [32, P])
        table_sink = sb("table_sink", [P, 1])
        stat = sb("stat", [P, 4, 4])
        poolw = sb("poolw", [P, 4, P])
        arena = place[0]
        assert arena + 69 * 1024 <= nc.sbuf_usable_end, (arena, nc.sbuf_usable_end)

        K = 1024
        squared = [at(f"squared{n}", [P, KT, T], F32, arena + first * K) for n, first in enumerate((40, 60, 60, 60, 60))]
        ada_first = [at(f"ada_first{k}", [P, 2048], F32, arena + 8 * k * K)[:] for k in range(5)]
        ada_first += [ada_raw[:].rearrange("p s n -> p (s n)"), mod_acc[:, 2048:4096],
                      work[:].rearrange("p k t -> p (k t)")]
        x_tok = at("x_tok", [P, TT, D], F32, arena + 40 * K)
        rows_a = at("rows_a", [104, P], F32, arena + 48 * K)
        rows_b = at("rows_b", [93, P], F32, arena + 49 * K)
        rows_c = at("rows_c", [3 * FT, 2, P], F32, arena + 50 * K)
        nflip = at("nflip", [P, NA_HEADS, 6, GRID_W], F32, arena + 56 * K)
        ze = at("ze", [P, N_EI, 512], F32, arena)
        nbias = at("nbias", [P, NA_HEADS, 6, GRID_W], F32, arena + 32 * K)
        ns = at("ns", [P, 4, T], F32, arena + 44 * K)
        npt = at("npt", [P, 2, TT * P], F32, arena + 48 * K)
        ntok = at("ntok", [P, 2, P], F32, arena + 50 * K)
        diag = at("diag", [P, A_HEADS * TT, SB], F32, arena + 20 * K)
        gk = at("gk", [P, 2, A_HEADS * T], F32, arena + 60 * K)
        att = at("att", [P, A_HEADS, TT, T], F32, arena + 32 * K)
        gex = [at("gex0", [P, A_HEADS * T], F32, arena + 40 * K)[:], at("gex1", [P, A_HEADS * T], F32, arena + 22 * K)[:]]
        gq_l = [at(f"gq_l{n}", [P, 2, A_HEADS * T], F32, a)[:] for n, a in enumerate((h_at, arena + 44 * K))]
        gk_l = [at(f"gk_l{n}", [P, 2, A_HEADS * T], F32, a)[:] for n, a in enumerate((h_at + 8 * K, arena + 52 * K))]
        hid_hi = at("hid_hi", [P, FT, T], F32R, arena)
        hid_lo = at("hid_lo", [P, FT, T], F32R, arena + 22 * K)
        conv = at("conv", [P, 2, T], F32, arena + 44 * K)
        gated = at("gated", [P, 2, T], F32, arena + 46 * K)
        hid = at("hid", [P, 2, T], F32, arena + 48 * K)
        zo = at("zo", [P, N_OI, 512], F32, arena)
        wrap_hi = at("wrap_hi", [P, KT, 2 * 64], F32R, arena + 40 * K)
        wrap_lo = at("wrap_lo", [P, KT, 2 * 64], F32R, arena + 44 * K)
        cs = at("cs", [P, 4, ROW], F32, arena + 40 * K)
        cpt = at("cpt", [P, 2, ROW], F32, arena + 46 * K)
        ctok = at("ctok", [P, 2, P], F32, arena + 49 * K)
        PADW = T + 16
        pu = at("pu", [P, 4, PADW], F32, arena + 52 * K)
        pw = [at(f"pw{w}", [P, 4, PADW], F32, arena + 52 * K + (n + 1) * 4352) for n, w in enumerate((2, 4, 8))]
        pmean = at("pmean", [P, 4, T], F32, arena + 52 * K)
        y_tok = at("y_tok", [P, TT, D], F32, arena + 52 * K)

        acc = ctx.enter_context(nc.psum_tensor("acc", [P, 2, 512], F32))
        big = ctx.enter_context(nc.psum_tensor("big", [P, 4, 512], F32))
        aux = ctx.enter_context(nc.psum_tensor("aux", [P, 2, 512], F32))

        diag_banks = [aux[:, 0], aux[:, 1], acc[:, 0], acc[:, 1]]
        ident = consts[:, C_ID:C_ID + P]
        mean_w = consts[:, C_MEAN:C_MEAN + P]
        hmean_w = consts[:, C_HMEAN:C_HMEAN + P]
        qT = ze[:, 0:2, :].rearrange("p u n -> p (u n)")
        fT = [ze[:, 2:4, :].rearrange("p u n -> p (u n)"), ze[:, 4:6, :].rearrange("p u n -> p (u n)")]
        gT = ze[:, 8:10, :].rearrange("p u n -> p (u n)")

        s_ident, s_const, s_x, s_rows = sem("s_ident"), sem("s_const"), sem("s_x"), sem("s_rows")
        bias_turned, bias_kept = sem("bias_turned"), sem("bias_kept")
        s_bias, s_poolw, s_out = sem("s_bias"), sem("s_poolw"), sem("s_out")
        first_landed = [sem(f"first_landed{k}") for k in range(KT)]
        w_landed = [sem(f"w_landed{i}") for i in range(RAW)]
        s_hi, s_lo, w_used = sem("s_hi"), sem("s_lo"), sem("w_used")
        ada_landed = [sem(f"ada_landed{i}") for i in range(2)]
        rest_landed = [sem(f"rest_landed{i}") for i in range(2)]
        ada_used, acc_zeroed, mod_summed, mod_ready = sem("ada_used"), sem("acc_zeroed"), sem("mod_summed"), sem("mod_ready")
        rows_turned, vecs_ready, x_turned, x_ready, cact_ready = (
            sem("rows_turned"), sem("vecs_ready"), sem("x_turned"), sem("x_ready"), sem("cact_ready"))
        gain_ready, norm_sq, norm_sum, rstd_ready, norm_mul, h_hi_ready, h_lo_ready = (
            sem("gain_ready"), sem("norm_sq"), sem("norm_sum"), sem("rstd_ready"), sem("norm_mul"), sem("h_hi_ready"),
            sem("h_lo_ready"))
        rms_ready, gla_rms = sem("rms_ready"), sem("gla_rms")
        z_evicted, x_updated, dve_chain = sem("z_evicted"), sem("x_updated"), sem("dve_chain")
        conv_mid, conv_taps, silu_ready, hid_ready, hid_hi_ready, hid_lo_ready = (
            sem("conv_mid"), sem("conv_taps"), sem("silu_ready"), sem("hid_ready"), sem("hid_hi_ready"),
            sem("hid_lo_ready"))
        scored, shifted, exp_done, turned, probs_kept, attended, out_taken, out_turned, out_placed = (
            sem("scored"), sem("shifted"), sem("exp_done"), sem("turned"), sem("probs_kept"), sem("attended"),
            sem("out_taken"), sem("out_turned"), sem("out_placed"))
        wrapped = sem("wrapped")
        lb_diff, lb_exp, lb_ready, gate_act, gates_ready, gla_done, diag_taken, att_copied, att_ready = (
            sem("lb_diff"), sem("lb_exp"), sem("lb_ready"), sem("gate_act"), sem("gates_ready"), sem("gla_done"), sem("diag_taken"),
            sem("att_copied"), sem("att_ready"))
        gla_out, gla_sq, gla_mean, gla_normed, gla_cleared = (
            sem("gla_out"), sem("gla_sq"), sem("gla_mean"), sem("gla_normed"), sem("gla_cleared"))
        gla_ready = [sem("gla_ready_back"), sem("gla_ready_ahead")]
        down_summed, mod_gathered, mod_kept = sem("down_summed"), sem("mod_gathered"), sem("mod_kept")
        pool_step, pool_mixed, pool_taken = sem("pool_step"), sem("pool_mixed"), sem("pool_taken")
        y_ready, y_turned, y_copied = sem("y_ready"), sem("y_turned"), [sem(f"y_copied{t}") for t in range(TT)]

        def stream(eng, first, count, unroll, step):
            trips = count // unroll
            if trips > 1:
                with eng.Fori(0, trips) as i:
                    for j in range(unroll):
                        step(i, first + j)
            elif trips == 1:
                for j in range(unroll):
                    step(0, first + j)
            for j in range(trips * unroll, count):
                step(0, first + j)

        def gla_level(eng, d, h, link):
            inc, exc = fT[d], gex[d]
            halves = lambda a: a.rearrange("p (b two h) -> p b two h", two=2, h=h)
            qs, ks = (1, 0) if d == 0 else (0, 1)
            n = LEVELS.index(h)
            if n >= 2:
                eng.wait_ge(gla_done, 2 * n - 2 + d)
            q = eng.tensor_tensor(halves(gq_l[n % 2][:, d, :])[:, :, qs, :], halves(qT)[:, :, qs, :],
                                  halves(inc)[:, :, qs, :], ALU.mult)
            if h == 1:
                q.then_inc(gla_ready[d], 1)
            else:
                eng.tensor_tensor(halves(gk_l[n % 2][:, d, :])[:, :, ks, :], halves(gk[:, d, :])[:, :, ks, :],
                                  halves(exc)[:, :, ks, :], ALU.mult).then_inc(gla_ready[d], 1)
            eng.wait_ge(gla_ready[d], n + 1 + (d == 0))
            if h < 128:
                edge = h - 1 if d == 0 else 0
                nb = A_HEADS * T // (2 * h)
                total = halves(inc)[:, :, qs, edge:edge + 1].to_broadcast([P, nb, h])
                link(eng.tensor_tensor(halves(exc)[:, :, ks, :], halves(exc)[:, :, ks, :], total, ALU.mult))
                before = halves(inc)[:, :, ks, edge:edge + 1].to_broadcast([P, nb, h])
                link(eng.tensor_tensor(halves(inc)[:, :, qs, :], halves(inc)[:, :, qs, :], before, ALU.mult))

        block = ctx.enter_context(nc.Block())

        @block.sync
        def _(sp):
            sp.dma_start(consts[:, :C_HMEAN], consts_in[:, :C_HMEAN]).then_inc(s_ident, 16)
            sp.dma_start(x_tok[:], x.rearrange("b (t p) d -> p (b t) d", p=P)).then_inc(s_x, 16)
            sp.dma_start(ada_first[0], ada_w[0, 0:P, 0:2048]).then_inc(first_landed[0], 16)
            sp.dma_start(rows_a[0:8, :], c.rearrange("o (k p) -> (o k) p", p=P)).then_inc(s_rows, 16)
            sp.dma_start(rows_a[8:104, :], ada_b.rearrange("l (k p) -> (l k) p", p=P)).then_inc(s_rows, 16)
            sp.dma_start(rows_b[0:16, :], norm_mix_g.rearrange("l (k p) -> (l k) p", p=P)).then_inc(s_rows, 16)
            sp.dma_start(rows_b[16:32, :], norm_ffn_g.rearrange("l (k p) -> (l k) p", p=P)).then_inc(s_rows, 16)
            sp.dma_start(rows_b[32:40, :], final_norm_g.rearrange("(k p) -> k p", p=P)).then_inc(s_rows, 16)
            sp.dma_start(rows_b[40:44, :], pool_scale.rearrange("o (k p) -> (o k) p", p=P)).then_inc(s_rows, 16)
            sp.dma_start(rows_b[44:48, :], hgrn_lb_logits.rearrange("o (k p) -> (o k) p", p=P)).then_inc(s_rows, 16)
            sp.dma_start(rows_b[48:49, :], hgrn_norm_g).then_inc(s_rows, 16)
            sp.dma_start(rows_b[49:93, :], ffn_conv_b.rearrange("l (k p) -> (l k) p", p=P)).then_inc(s_rows, 16)
            for l in (0, 1):
                sp.dma_start(rows_c[:, l, :], ffn_conv_w[l].rearrange("j (k p) -> (j k) p", p=P)).then_inc(s_rows, 16)
            for k in range(1, KT):
                sp.dma_start(ada_first[k], ada_w[0, k * P:(k + 1) * P, 0:2048]).then_inc(first_landed[k], 16)
            def load(i, n, src, halves_of="k"):
                if not (isinstance(i, int) and 4 * i + n < RAW):
                    sp.wait_ge(s_lo, i * 8 + 2 * (n - RAW + 1))
                slot = n % RAW
                if halves_of == "k":
                    k = src.shape[1]
                    dst = w_raw[:, slot, :].rearrange("p (k n) -> p k n", k=k)
                    for part in (slice(0, k // 2), slice(k // 2, k)):
                        sp.dma_start(dst[:, part, :], src[:, part, :]).then_inc(w_landed[slot], 16)
                else:
                    dst = w_raw[:, slot, :].rearrange("p (k h n) -> p k h n", k=KT, h=2)
                    for h in (0, 1):
                        sp.dma_start(dst[:, :, h, :], src[:, :, h, :]).then_inc(w_landed[slot], 16)

            def columns(w):
                return w.rearrange("(k p) n -> p k n", p=P)

            def project(w, first, count, skip=0):
                stream(sp, first + skip, count - skip, 4,
                       lambda i, n: load(i, n, columns(w)[:, :, bass.ds(i * 1024 + (n - first) * 256, 256)]))

            def up(l, first):
                w = ffn_w_up[l].rearrange("(k p) (h n) -> p k h n", p=P, h=2)
                stream(sp, first, N_UP, 4, 
                       lambda i, n: load(i, n, w[:, :, :, bass.ds(i * 512 + (n - first) * P, P)], "h"))

            def down(l, first):
                w = ffn_w_down[l].rearrange("(u k p) n -> u p k n", p=P, k=2)
                stream(sp, first, N_DN, 4, lambda i, n: load(i, n, w[bass.ds(i * 4 + (n - first), 1)]
                                                             .rearrange("u p k n -> p (u k) n")))

            project(even_w_in[0], EI, 4)
            project(even_w_in[0], EI, 6, skip=4)
            sp.dma_start(consts[:, C_HMEAN:], consts_in[:, C_HMEAN:]).then_inc(s_const, 16)
            rpb_rows = 2 * NA_KC - 1
            for rr in (0, 1):
                first = (NA_KR - 1 - 2 - rr) * rpb_rows + NA_KC - 1 - (GRID_W - 1)
                for h in range(NA_HEADS):
                    src = bass.AP(na_rpb.tensor, na_rpb.offset + first + h * (2 * NA_KR - 1) * rpb_rows,
                                  [[1, GRID_W], [rpb_rows, 6], [1, GRID_W]])
                    sp.dma_start(nflip[rr * GRID_W:(rr + 1) * GRID_W, h], src).then_inc(s_bias, 16)
                project(even_w_in[0], EI, 7 + rr, skip=6 + rr)
            sp.dma_start(poolw[:], pool_w[0].rearrange("g c d -> c g d")).then_inc(s_poolw, 16)
            project(even_w_in[0], EI, N_EI, skip=8)
            project(even_w_out[0], EO, N_EO)
            for tile in range(20, 32):
                sp.wait_ge(ada_used, ADA1 + tile - 1)
                k, q, slot = tile // 4, tile % 4, tile % 2
                sp.dma_start(ada_raw[:, slot, :], ada_w[0, k * P:(k + 1) * P, 2048 + q * 1024:3072 + q * 1024]).then_inc(
                    rest_landed[slot], 16)
            up(0, UP0)
            down(0, DN0)
            project(odd_w_in[0], OI, N_OI)
            project(odd_w_out[0], OO, N_OO)
            up(1, UP1)
            down(1, DN1)
            for t in range(TT):
                sp.wait_ge(y_copied[t], 1)
                sp.dma_start(out[0, t * P:(t + 1) * P, :], y_tok[:, t, :]).then_inc(s_out, 16)
            sp.wait_ge(s_out, 16 * TT)

        @block.gpsimd
        def _(pool):
            def tile_in(l, k, q, slot, i2, t2):
                pool.wait_ge(ada_used, i2 * 2 + 2 * t2 + slot - 1)
                src = ada_w[l].rearrange("(k p) n -> k p n", p=P)[bass.ds(k, 1), :, q:q + 1024]
                pool.dma_start(ada_raw[:, slot, :], src.rearrange("k p n -> p (k n)")).then_inc(ada_landed[slot], 16)

            def head(l, base):
                tile_in(l, 0, 0, 0, 0, base // 2)
                tile_in(l, 0, 1024, 1, 0, base // 2)
                with pool.Fori(1, KT) as k:
                    for q in (0, 1):
                        tile_in(l, k, q * 1024, q, k, base // 2)

            def rest(l, base, first=0, last=KT):
                with pool.Fori(first, last) as k:
                    for q in range(4):
                        tile_in(l, k, 2048 + q * 1024, q % 2, k * 2, base // 2 + q // 2)

            done = [0]

            def link(ins):
                done[0] += 1
                ins.then_inc(pool_step, 1)
                pool.wait_ge(pool_step, done[0])

            pool.wait_ge(mod_gathered, 1)
            pool.memset(mod_acc[:], 0.0).then_inc(acc_zeroed, 1)
            rest(0, ADA1, 0, 5)
            pool.wait_ge(lb_ready, 1)
            pool.wait_ge(gate_act, 4)
            for d in (0, 1):
                for h in range(A_HEADS):
                    cols = slice(h * T, (h + 1) * T)
                    pool.tensor_scalar(fT[d][:, cols], fT[d][:, cols], lbt[:, 5, h:h + 1], lbt[:, 4, h:h + 1],
                                       ALU.mult, ALU.add)
                    ins = pool.tensor_scalar(gk[:, d, cols], gk[:, d, cols], lbt[:, 5, h:h + 1], None, ALU.mult)
            ins.then_inc(gates_ready, 1)
            pool.wait_ge(z_evicted, N_EI)
            for factors in (gq_l[0], gk_l[0], gk_l[1]):
                pool.memset(factors, 0.0).then_inc(gla_cleared, 1)
            pool.wait_ge(out_placed, STEPS // 2)
            pool.memset(gex[1], 1.0).then_inc(gla_cleared, 1)
            pool.wait_ge(gates_ready, 1)
            pool.wait_ge(gla_cleared, 5)
            pool.wait_ge(gate_act, 5)
            for h in LEVELS:
                if h == 2:
                    pool.wait_ge(gla_cleared, 6)
                gla_level(pool, 1, h, link)
            pool.wait_ge(mod_gathered, 2)
            pool.memset(mod_acc[:], 0.0).then_inc(acc_zeroed, 1)
            head(1, ADA2)
            pool.wait_ge(mod_gathered, 3)
            pool.memset(mod_acc[:], 0.0).then_inc(acc_zeroed, 1)
            rest(1, ADA3)
            pool.wait_ge(z_evicted, N_EI + N_OI)
            u = zo[:, 18:20, :].rearrange("p u (g t) -> p (u g) t", g=2)
            link(pool.memset(pu[:], 0.0))
            link(pool.tensor_copy(pu[:, :, 8:8 + T], u))
            s2, s4, s8 = pw
            link(pool.tensor_tensor(s2[:, :, 1:272], pu[:, :, 0:271], pu[:, :, 1:272], ALU.add))
            link(pool.tensor_tensor(s4[:, 1:4, 2:271], s2[:, 1:4, 1:270], s2[:, 1:4, 3:272], ALU.add))
            link(pool.tensor_tensor(s8[:, 2:4, 4:269], s4[:, 2:4, 2:267], s4[:, 2:4, 6:271], ALU.add))
            link(pool.tensor_tensor(s4[:, 3, 8:264], s8[:, 3, 4:260], s8[:, 3, 12:268], ALU.add))
            for g, s in enumerate((s2, s4, s8, s4)):
                link(pool.tensor_tensor(pmean[:, g, :], s[:, g, 8:8 + T], consts[:, C_INV + g * T:C_INV + (g + 1) * T],
                                        ALU.mult))
            pool.tensor_tensor(pmean[:], pmean[:], u, ALU.subtract).then_inc(pool_step, 1)

        POOL_STEPS = 2 * (len(LEVELS) - 1) + 11

        @block.scalar
        def _(act):
            def split_hi(i, n):
                if isinstance(i, int) and n >= UNITS:
                    return
                if not isinstance(i, int) or n >= SPLIT:
                    act.wait_ge(w_used, i * 4 + n - SPLIT + 1)
                act.wait_ge(w_landed[n % RAW], (i + n // RAW + 1) * 32)
                for half in (0, 1):
                    part = slice(half * UNIT // 2, (half + 1) * UNIT // 2)
                    nc.scalar.activation(w_hi[:, n % SPLIT, part], w_raw[:, n % RAW, part], ACT.Copy).then_inc(s_hi, 1)

            def squares(idx, first=0, last=KT):
                for k in range(first, last):
                    if idx == 0:
                        act.wait_ge(x_ready, k // 2 + 1)
                    else:
                        act.wait_ge(x_updated, KT * (idx - 1) + k + 1)
                    nc.scalar.activation(squared[idx][:, k, :], xT[:, k, :], ACT.Square).then_inc(norm_sq, 1)

            def rms(idx):
                act.wait_ge(norm_sum, idx + 1)
                nc.scalar.activation(rstd[:], aux[:, 0, 0:T], ACT.Sqrt, bias=consts[:, C_EPS:C_EPS + 1]).then_inc(
                    rms_ready, 1)

            def norm(idx, shift):
                for k in range(KT):
                    act.wait_ge(norm_mul, idx * KT + k + 1)
                    nc.scalar.activation(h_hi[:, k, :], work[:, k, :], ACT.Identity,
                                         bias=shift[:, k:k + 1]).then_inc(h_hi_ready, 1)

            def preload_sqrt():
                nc.scalar.activation(table_sink[:], consts[:, C_EPS:C_EPS + 1], ACT.Sqrt)

            act.wait_ge(rows_turned, 1)
            nc.scalar.activation(vecs[:, 0:V_ALL], aux[:, 0, 0:V_ALL], ACT.Copy).then_inc(vecs_ready, 1)
            act.wait_ge(vecs_ready, 1)
            nc.scalar.activation(cact[:], vecs[:, V_C:V_C + KT], ACT.Silu).then_inc(cact_ready, 1)
            for b in range(4):
                act.wait_ge(x_turned, b + 1)
                nc.scalar.activation(xT[:, 2 * b:2 * b + 2, :].rearrange("p k t -> p (k t)"), big[:, b, :],
                                     ACT.Copy).then_inc(x_ready, 1)
            act.wait_ge(s_ident, 16)
            squares(0)
            rms(0)
            split_hi(0, 0)
            split_hi(0, 1)
            norm(0, mods[:, 0, 0:8])

            def in_step(first, zbuf, scale):
                def step(i, n):
                    act.wait_ge(w_used, i * 4 + n + 1)
                    to = zbuf[:, bass.ds(i * 4 + (n - first), 1), :].rearrange("p u n -> p (u n)")
                    nc.scalar.activation(to, acc[:, (n - first) % 2, :], ACT.Copy, scale=scale).then_inc(z_evicted, 1)
                    if isinstance(i, int) and n + SPLIT in (EO, EO + 1):
                        return
                    split_hi(i, n + SPLIT)
                return step

            stream(act, EI, 12, 4, in_step(EI, ze, 1.0))
            act.wait_ge(lb_diff, 1)
            nc.scalar.activation(lbt[:, 1, :], lbt[:, 0, :], ACT.Exp).then_inc(lb_exp, 1)
            act.wait_ge(z_evicted, 10)
            act.wait_ge(bias_kept, 6)
            for n in range(EI + 12, EI + N_EI):
                in_step(EI, ze, 1.0)(0, n)
                d = n - EI - 12
                if d < 2:
                    nc.scalar.activation(gk[:, d, :], fT[d], ACT.Sigmoid, scale=-1.0).then_inc(gate_act, 1)
                    act.wait_ge(gate_act, 2 * d + 1)
                    nc.scalar.activation(fT[d], fT[d], ACT.Sigmoid).then_inc(gate_act, 1)
                elif d == 2:
                    nc.scalar.activation(qT, qT, ACT.Silu).then_inc(gate_act, 1)

            def attend(base, scores, kept, tokens, placed, beside=lambda s: None):
                width = scores.shape[2]
                for s in range(STEPS + 7):
                    if s < STEPS:
                        act.wait_ge(shifted, base + s + 1)
                        nc.scalar.activation(scores[:, s % 4, :], scores[:, s % 4, :], ACT.Exp,
                                             bias=stat[:, s % 4, 1:2], accum_out=stat[:, s % 4, 2:3]).then_inc(exp_done, 1)
                    if 0 <= s - 2 < STEPS:
                        r = s - 2
                        act.wait_ge(turned, base + r + 1)
                        if r >= 2:
                            act.wait_ge(attended, base + r - 1)
                        nc.scalar.activation(kept[:, r % 2, :], aux[:, r % 2, 0:width], ACT.Copy).then_inc(probs_kept, 1)
                    if s >= 7 and (s - 6) % 2:
                        j = (s - 6) // 2
                        act.wait_ge(out_turned, base // 2 + j + 1)
                        nc.scalar.activation(placed(j), tokens(big[:, 3, 0:P]), ACT.Copy).then_inc(out_placed, 1)
                    beside(s)

            attend(0, ns, npt, lambda a: a, lambda j: work[:, 4 + j // 2, (j % 2) * P:(j % 2 + 1) * P])
            nc.scalar.activation(gT, gT, ACT.Silu).then_inc(gate_act, 1)
            preload_sqrt()
            act.wait_ge(gla_done, len(GLA_STEPS))
            flat = att[0:SB].rearrange("p h t n -> p h (t n)")
            for cols in (slice(SB, 6 * SB), slice(7 * SB, 8 * SB)):
                nc.scalar.activation(flat[:, :, cols], big[0:SB, :, cols], ACT.Copy).then_inc(att_copied, 1)
            act.wait_ge(out_placed, STEPS // 2)
            nc.scalar.activation(h_hi[:, 4:8, :], work[:, 4:8, :], ACT.Copy).then_inc(h_hi_ready, 1)
            split_hi(0, EO)
            for b in (0, 1):
                act.wait_ge(gla_out, b + 1)
                nc.scalar.activation(work[:, 2 * b:2 * b + 2, :].rearrange("p k t -> p (k t)"), acc[:, b, :],
                                     ACT.Copy).then_inc(gla_sq, 1)
                nc.scalar.activation(gq_l[1][:, 0, b * 512:(b + 1) * 512], acc[:, b, :], ACT.Square).then_inc(gla_sq, 1)
            for b in (0, 1):
                act.wait_ge(gla_mean, b + 1)
                nc.scalar.activation(gk_l[1][:, 0, b * 512:(b + 1) * 512], aux[:, b, :], ACT.Sqrt,
                                     bias=consts[:, C_EPS:C_EPS + 1]).then_inc(gla_rms, 1)
            split_hi(0, EO + 1)
            act.wait_ge(gla_normed, 2)
            nc.scalar.activation(h_hi[:, 0:4, :], work[:, 0:4, :], ACT.Copy).then_inc(h_hi_ready, 1)

            def out_projection(first, idx):
                for n in range(first, first + N_EO):
                    if n < first + N_EO - 1:
                        split_hi(0, n + SPLIT)
                    squares(idx, 2 * (n - first), 2 * (n - first) + 2)
                rms(idx)
                split_hi(0, first + N_EO - 1 + SPLIT)

            def ffn(l, first_up, first_down, idx):
                norm(idx, mods[:, l, 24:32])

                def up_step(i, n):
                    u = n - first_up
                    a = u % 2
                    nu = i * 4 + (l * FT + u)
                    act.wait_ge(w_used, i * 4 + n + 1)
                    nc.scalar.activation(conv[:, a, :], acc[:, a, 0:T], ACT.Identity,
                                         bias=vecs[:, bass.ds(i * 4 + (V_CB + l * FT + u), 1)],
                                         scale=vecs[:, bass.ds(i * 4 + (V_CW + l * 3 * FT + FT + u), 1)]
                                         ).then_inc(conv_mid, 1)
                    split_hi(i, n + SPLIT)
                    act.wait_ge(conv_taps, nu * 2 + 2)
                    nc.scalar.activation(gated[:, a, :], conv[:, a, :], ACT.Silu).then_inc(silu_ready, 1)
                    act.wait_ge(hid_ready, nu + 1)
                    nc.scalar.activation(hid_hi[:, bass.ds(i * 4 + u, 1), :].rearrange("p u n -> p (u n)"),
                                         hid[:, a, :], ACT.Copy).then_inc(hid_hi_ready, 1)
                stream(act, first_up, N_UP, 4, up_step)
                preload_sqrt()
                stream(act, first_down, N_DN, 4, lambda i, n: split_hi(i, n + SPLIT)) if l == 0 else \
                    stream(act, first_down, N_DN - SPLIT, 4, lambda i, n: split_hi(i, n + SPLIT))

            out_projection(EO, 1)
            ffn(0, UP0, DN0, 1)

            squares(2)
            rms(2)
            norm(2, mods[:, 1, 0:8])
            stream(act, OI, 6, 4, in_step(OI, zo, SCALE))
            act.wait_ge(h_lo_ready, NORM_AT[2] + KT)
            for to, frm in ((wrap_hi, h_hi), (wrap_lo, h_lo)):
                nc.scalar.activation(to[:, :, 0:64], frm[:, :, 3 * 64:4 * 64].bitcast(F32), ACT.Copy).then_inc(wrapped, 1)
                nc.scalar.activation(to[:, :, 64:128], frm[:, :, 0:64].bitcast(F32), ACT.Copy).then_inc(wrapped, 1)
            stream(act, OI + 6, 8, 4, in_step(OI, zo, 1.0))
            for n in range(OI + 14, OI + 18):
                u = n - OI
                a = u % 2
                act.wait_ge(w_used, n + 1)
                for side in (0, 1):
                    lane = slice(64 * side, 64 * side + 64)
                    for t in range(TT):
                        residue = (2 * t + side + (0 if u < 16 else 1)) % RES
                        ins = nc.scalar.activation(zo[lane, 14 + residue, a * 256:(a + 1) * 256],
                                                   acc[lane, a, t * T:(t + 1) * T], ACT.Copy)
                ins.then_inc(z_evicted, 1)
                split_hi(0, n + SPLIT)
            for n in range(OI + 18, OI + N_OI):
                act.wait_ge(w_used, n + 1)
                nc.scalar.activation(zo[:, n - OI, :].rearrange("p (g b r) -> p g r b", g=2, r=RES),
                                     acc[:, n % 2 ^ OI % 2, :].rearrange("p (g r b) -> p g r b", g=2, r=RES),
                                     ACT.Copy).then_inc(z_evicted, 1)

            by_residue = lambda a: a.rearrange("p (b r) -> p r b", r=RES)
            attend(STEPS, cs, cpt, lambda a: a.rearrange("p (r b) -> p r b", r=2),
                   lambda j: by_residue(work[:, j // 2, :])[:, 2 * (j % 2):2 * (j % 2) + 2, :],
                   lambda s: split_hi(0, OO + s // 4 - 1) if s in (4, 8) else None)
            preload_sqrt()
            act.wait_ge(out_placed, STEPS)
            nc.scalar.activation(h_hi[:, 0:4, :], work[:, 0:4, :], ACT.Copy).then_inc(h_hi_ready, 1)
            act.wait_ge(pool_mixed, 1)
            for g in range(4):
                nc.scalar.activation(work[:, 4 + g, :], big[:, g // 2, (g % 2) * T:(g % 2 + 1) * T], ACT.Copy,
                                     scale=vecs[:, V_PSC + g:V_PSC + g + 1]).then_inc(pool_taken, 1)
            act.wait_ge(pool_taken, 4)
            nc.scalar.activation(h_hi[:, 4:8, :], work[:, 4:8, :], ACT.Copy).then_inc(h_hi_ready, 1)
            out_projection(OO, 3)
            ffn(1, UP1, DN1, 3)

            squares(4)
            rms(4)
            act.wait_ge(y_turned, 1)
            nc.scalar.activation(y_tok[:, 0, :], big[:, 0:2, :].rearrange("p b n -> p (b n)"), ACT.Copy).then_inc(y_copied[0], 1)

        @block.vector
        def _(dve):
            chained = [0]

            def link(ins):
                chained[0] += 1
                ins.then_inc(dve_chain, 1)
                dve.wait_ge(dve_chain, chained[0])

            def split_lo(i, n):
                if isinstance(i, int) and n >= UNITS:
                    return
                for half in (0, 1):
                    part = slice(half * UNIT // 2, (half + 1) * UNIT // 2)
                    dve.wait_ge(s_hi, i * 8 + 2 * n + half + 1)
                    dve.tensor_tensor(w_lo[:, n % SPLIT, part], w_raw[:, n % RAW, part],
                                      w_hi[:, n % SPLIT, part].bitcast(F32), ALU.subtract).then_inc(s_lo, 1)

            def add_tile(k, q, slot, i2, t2, landed=ada_landed, before=ADA1):
                dve.wait_ge(ada_used, i2 * 2 + 2 * t2 + slot - 1)
                if before == ADA1 and t2 >= ADA2 // 2:
                    before += 12
                dve.wait_ge(landed[slot], (i2 + t2 + 1 - before // 2) * 16)
                sums = mod_acc[:, q * 1024:(q + 1) * 1024]
                dve.scalar_tensor_tensor(out=sums, in0=ada_raw[:, slot, :], scalar=cact[:, bass.ds(k, 1)], in1=sums,
                                         op0=ALU.mult, op1=ALU.add).then_inc(ada_used, 1)

            def keep_mods(e, count, bank):
                dve.wait_ge(mod_gathered, e + 1)
                dve.tensor_copy(mod_rows[0:count, :], bank[0:count, 0:P]).then_inc(mod_kept, 1)

            def take_mods(e, l, first, count, bank):
                dve.wait_ge(mod_summed, e + 1)
                cols = slice(V_ADAB + 48 * l + first, V_ADAB + 48 * l + first + count)
                dve.tensor_tensor(mods[:, l, first:first + count], bank[:, P:P + count], vecs[:, cols],
                                  ALU.add).then_inc(mod_ready, 1)
                dve.wait_ge(mod_ready, e + 1)

            def make_gain(idx, l, first, v):
                dve.scalar_tensor_tensor(out=gain[:, idx, :], in0=mods[:, l, first:first + KT], scalar=1.0,
                                         in1=vecs[:, v:v + KT], op0=ALU.add, op1=ALU.mult).then_inc(gain_ready, 1)

            def reciprocal_rms(idx):
                dve.wait_ge(rms_ready, idx + 1)
                dve.reciprocal(rstd[:], rstd[:]).then_inc(rstd_ready, 1)
                dve.wait_ge(rstd_ready, idx + 1)

            def norm(idx, shift, order=lambda a: (a, a)):
                if idx:
                    reciprocal_rms(idx)
                dve.wait_ge(gain_ready, idx + 1)
                for step in range(KT + 2):
                    if step < KT:
                        dve.scalar_tensor_tensor(out=order(work[:, step, :])[0], in0=order(xT[:, step, :])[1],
                                                 scalar=gain[:, idx, step:step + 1], in1=order(rstd[:])[1], op0=ALU.mult,
                                                 op1=ALU.mult).then_inc(norm_mul, 1)
                    if step < 2:
                        continue
                    k = step - 2
                    dve.wait_ge(h_hi_ready, NORM_AT[idx] + k + 1)
                    dve.scalar_tensor_tensor(out=h_lo[:, k, :], in0=work[:, k, :], scalar=shift[:, k:k + 1],
                                             in1=h_hi[:, k, :].bitcast(F32), op0=ALU.add,
                                             op1=ALU.subtract).then_inc(h_lo_ready, 1)

            def mixed_lo(value, half):
                part = slice(4 * half, 4 * half + 4)
                dve.wait_ge(h_hi_ready, value)
                dve.tensor_tensor(h_lo[:, part, :], work[:, part, :], h_hi[:, part, :].bitcast(F32),
                                  ALU.subtract).then_inc(h_lo_ready, 1)

            dve.wait_ge(cact_ready, 1)
            sums = mod_acc[:, 0:2048]
            for k in range(KT):
                dve.wait_ge(first_landed[k], 16)
                if k == 0:
                    dve.tensor_scalar(sums, ada_first[k], cact[:, 0:1], None, ALU.mult).then_inc(ada_used, 1)
                else:
                    dve.wait_ge(ada_used, k)
                    dve.scalar_tensor_tensor(out=sums, in0=ada_first[k], scalar=cact[:, k:k + 1], in1=sums,
                                             op0=ALU.mult, op1=ALU.add).then_inc(ada_used, 1)
            reciprocal_rms(0)
            split_lo(0, 0)
            keep_mods(0, 16, aux[:, 1])
            take_mods(0, 0, 0, 16, aux[:, 1])
            make_gain(0, 0, 8, V_NMIX)
            norm(0, mods[:, 0, 0:8])
            split_lo(0, 1)
            logits = vecs[:, V_LB:V_LB + A_HEADS]
            dve.tensor_tensor(lbt[:, 0, :], logits, logits, ALU.subtract).then_inc(lb_diff, 1)

            dve.wait_ge(acc_zeroed, 1)

            def in_step(first, base, tile0, per):
                def step(i, n):
                    if not (isinstance(i, int) and n + SPLIT in (EO, EO + 1, OO, OO + 1)):
                        split_lo(i, n + SPLIT)
                    for tile in range(tile0 + per * (n - first), tile0 + per * (n - first + 1)):
                        add_tile(i * per + tile // 4, tile % 4, tile % 2, i * 2 * per, base // 2 + tile // 2)
                return step
            def keep_bias(first, last):
                for b in range(first, last):
                    dve.wait_ge(bias_turned, b + 1)
                    mask = consts[:, C_NAT:C_NAT + GRID_W].unsqueeze(1).to_broadcast([P, 8, GRID_W])
                    dve.tensor_tensor(nbias[:].rearrange("p h e c -> p (h e) c")[:, 8 * b:8 * b + 8, :],
                                      big[:, b % 4, :].rearrange("p (e c) -> p e c", c=GRID_W), mask,
                                      ALU.add).then_inc(bias_kept, 1)

            stream(dve, EI, 8, 4, in_step(EI, ADA1, 0, 1))
            stream(dve, EI + 8, 2, 4, in_step(EI + 8, ADA1, 8, 2))
            dve.wait_ge(s_const, 16)
            keep_bias(0, 4)
            stream(dve, EI + 10, 2, 4, in_step(EI + 8, ADA1, 8, 2))
            keep_bias(4, 6)
            for n, tile, count in ((12, 16, 2), (13, 18, 1), (14, 19, 1), (15, 20, 0)):
                in_step(EI + n, ADA1, tile, count)(0, EI + n)
            dve.wait_ge(lb_exp, 1)
            link(dve.reciprocal(lbt[:, 2, :], lbt[:, 1, :]))
            link(dve.tensor_tensor(lbt[:, 3, :], lbt[:, 1, :], lbt[:, 2, :], ALU.mult))
            link(dve.tensor_tensor(lbt[:, 0, :], lbt[:, 3, :], lbt[:, 3, :], ALU.subtract))
            dve.tensor_scalar(lbt[:, 4, :], lbt[:, 0, :], LB_FLOOR, None, ALU.max)
            dve.tensor_scalar(lbt[:, 5, :], lbt[:, 0, :], -1.0, 1.0, ALU.mult, ALU.add).then_inc(lb_ready, 1)

            def attend(base, scores, tok, shift, beside=lambda s: None):
                for s in range(STEPS + 4):
                    if s >= 4:
                        r = s - 4
                        j = r // 2
                        dve.wait_ge(exp_done, base + r + 1)
                        link(dve.reciprocal(stat[:, r % 4, 3:4], stat[:, r % 4, 2:3]))
                        dve.wait_ge(attended, base + r + 1)
                        if r % 2 == 0 and j >= 2:
                            dve.wait_ge(out_turned, base // 2 + j - 1)
                        dve.tensor_scalar(tok[:, j % 2, (r % 2) * DH:(r % 2 + 1) * DH], acc[:, r % 2, 0:DH],
                                          stat[:, r % 4, 3:4], None, ALU.mult).then_inc(out_taken, 1)
                    if s < STEPS:
                        dve.wait_ge(scored, base + s + 1)
                        if s >= 4:
                            dve.wait_ge(turned, base + s - 3)
                        link(shift(s, 2 * (s // 4) + s % 2, s // 2 % 2))
                        link(dve.tensor_reduce(stat[:, s % 4, 0:1], scores[:, s % 4, :], AX_X, ALU.max))
                        dve.tensor_scalar(stat[:, s % 4, 1:2], stat[:, s % 4, 0:1], -1.0, None,
                                          ALU.mult).then_inc(shifted, 1)
                    beside(s)

            def nat_shift(s, h, t):
                e = 2 - 2 * t
                return dve.scalar_tensor_tensor(out=ns[:, s % 4, :], in0=big[:, s % 3, 0:T], scalar=SCALE,
                                                op0=ALU.mult, op1=ALU.add,
                                                in1=nbias[:, h, e:e + 4, :].rearrange("p e c -> p (e c)"))

            def dil_shift(s, h, t):
                for at0, at1, k in ((0, T, -slope(0, h)),
                                    (T, T + 64, consts[:, C_SLOPE + 2 * h:C_SLOPE + 2 * h + 1]),
                                    (T + 64, ROW, consts[:, C_SLOPE + 2 * h + 1:C_SLOPE + 2 * h + 2])):
                    col = C_DIST + t * ROW
                    ins = dve.scalar_tensor_tensor(out=cs[:, s % 4, at0:at1], in0=consts[:, col + at0:col + at1],
                                                   scalar=k, in1=big[:, s % 3, at0:at1], op0=ALU.mult, op1=ALU.add)
                return ins

            def add_rest(tile):
                add_tile(tile // 4, tile % 4, tile % 2, 0, (ADA1 + tile) // 2, rest_landed, ADA1 + 20)

            def later_tiles(s):
                if s < STEPS and s % 2:
                    add_rest(20 + s // 2)

            attend(0, ns, ntok, nat_shift, later_tiles)
            dve.wait_ge(out_placed, STEPS // 2)
            dve.memset(gex[0], 1.0).then_inc(gla_cleared, 1)

            def take_diag(s):
                d, h = GLA_STEPS[s]
                n = SMALL.index(s)
                dve.wait_ge(gla_done, s + 1)
                src = diag_banks[n % 4].rearrange("p (b q) -> p b q", q=SB)
                if h == 0:
                    dve.tensor_copy(diag[:], src).then_inc(diag_taken, 1)
                else:
                    dve.wait_ge(diag_taken, n)
                    col = C_LVL + (d * 6 + LEVELS.index(h)) * SB
                    mask = consts[:, col:col + SB].bitcast(I32).unsqueeze(1).to_broadcast([P, A_HEADS * TT, SB])
                    dve.copy_predicated(diag[:], mask, src).then_inc(diag_taken, 1)

            dve.wait_ge(gates_ready, 1)
            dve.wait_ge(gate_act, 5)
            dve.wait_ge(gla_cleared, 5)
            dve.tensor_tensor(gk_l[0][:, 0, :], gk[:, 0, :], gk[:, 1, :], ALU.add).then_inc(gla_ready[0], 1)
            for n, h in enumerate(LEVELS):
                if n == 1:
                    dve.wait_ge(gla_cleared, 6)
                gla_level(dve, 0, h, link)
                if n == 0:
                    dve.memset(gq_l[1], 0.0).then_inc(gla_cleared, 1)
                if n >= 4:
                    add_rest(24 + n)
                for s in ([0] if n == 0 else [2 * n - 1, 2 * n]):
                    if s in SMALL:
                        take_diag(s)
            dve.wait_ge(gla_done, len(GLA_STEPS))
            flat = att[SB:P].rearrange("p h t n -> p h (t n)")
            for cols in (slice(0, SB), slice(2 * SB, 7 * SB)):
                dve.tensor_copy(flat[:, :, cols], big[SB:P, :, cols])
            dve.wait_ge(diag_taken, len(SMALL))
            for q in range(P // SB):
                rows = slice(SB * q, SB * (q + 1))
                for t in range(TT):
                    ins = dve.tensor_copy(att[rows, :, t, t * P + SB * q:t * P + SB * (q + 1)],
                                          diag[rows].rearrange("p (h t) q -> p h t q", t=TT)[:, :, t, :])
            ins.then_inc(att_ready, 1)
            mixed_lo(MIX_AT[0] + 1, 1)
            split_lo(0, EO)
            for b in (0, 1):
                part = slice(b * 512, (b + 1) * 512)
                o = work[:, 2 * b:2 * b + 2, :].rearrange("p k t -> p (k t)")
                dve.wait_ge(gla_rms, b + 1)
                link(dve.reciprocal(gk_l[1][:, 0, part], gk_l[1][:, 0, part]))
                link(dve.scalar_tensor_tensor(out=o, in0=o, scalar=vecs[:, V_HG:V_HG + 1], in1=gk_l[1][:, 0, part],
                                              op0=ALU.mult, op1=ALU.mult))
                dve.wait_ge(gate_act, 6)
                dve.tensor_tensor(o, o, gT[:, part], ALU.mult).then_inc(gla_normed, 1)
            keep_mods(1, 32, big[:, 0])
            mixed_lo(MIX_AT[0] + 2, 0)
            split_lo(0, EO + 1)
            take_mods(1, 0, 16, 32, big[:, 0])
            make_gain(1, 0, 32, V_NFFN)

            def out_projection(l, first):
                for n in range(first, first + N_EO):
                    dve.wait_ge(w_used, n + 1)
                    for g in (0, 1):
                        k = 2 * (n - first) + g
                        dve.scalar_tensor_tensor(out=xT[:, k, :], in0=acc[:, (n - first) % 2, g * T:(g + 1) * T],
                                                 scalar=mods[:, l, 16 + k:17 + k], in1=xT[:, k, :], op0=ALU.mult,
                                                 op1=ALU.add).then_inc(x_updated, 1)
                    if n < first + N_EO - 1:
                        split_lo(0, n + SPLIT)

            def ffn(l, first_up, first_down, idx):
                norm(idx, mods[:, l, 24:32])
                split_lo(0, first_up + 1)
                if l == 0:
                    dve.wait_ge(acc_zeroed, 2)

                def up_step(adding):
                    def step(i, n):
                        u = n - first_up
                        a = u % 2
                        nu = i * 4 + (l * FT + u)
                        tap = lambda j: vecs[:, bass.ds(i * 4 + (V_CW + l * 3 * FT + j * FT + u), 1)]
                        dve.wait_ge(conv_mid, nu + 1)
                        dve.scalar_tensor_tensor(out=conv[:, a, 1:T], in0=acc[:, a, 0:T - 1], scalar=tap(0),
                                                 in1=conv[:, a, 1:T], op0=ALU.mult, op1=ALU.add).then_inc(conv_taps, 1)
                        dve.wait_ge(conv_taps, nu * 2 + 1)
                        dve.scalar_tensor_tensor(out=conv[:, a, 0:T - 1], in0=acc[:, a, 1:T], scalar=tap(2),
                                                 in1=conv[:, a, 0:T - 1], op0=ALU.mult, op1=ALU.add).then_inc(conv_taps, 1)
                        split_lo(i, n + SPLIT)
                        dve.wait_ge(silu_ready, nu + 1)
                        dve.tensor_tensor(hid[:, a, :], gated[:, a, :], acc[:, a, T:2 * T], ALU.mult).then_inc(hid_ready, 1)
                        if adding:
                            add_tile(i * 2 + u // 2, u % 2, u % 2, i * 2, ADA2 // 2 + u // 2)
                        dve.wait_ge(hid_hi_ready, nu + 1)
                        dve.tensor_tensor(hid_lo[:, bass.ds(i * 4 + u, 1), :].rearrange("p u n -> p (u n)"),
                                          hid[:, a, :],
                                          hid_hi[:, bass.ds(i * 4 + u, 1), :].rearrange("p u n -> p (u n)").bitcast(F32),
                                          ALU.subtract).then_inc(hid_lo_ready, 1)
                    return step
                if l == 0:
                    stream(dve, first_up, 16, 4, up_step(True))
                    for n in range(first_up + 16, first_up + N_UP):
                        up_step(False)(0, n)
                else:
                    stream(dve, first_up, N_UP, 4, up_step(False))
                stream(dve, first_down, N_DN if l == 0 else N_DN - SPLIT, 4, lambda i, n: split_lo(i, n + SPLIT))
                for k in range(KT):
                    if k < KT - 2:
                        dve.wait_ge(down_summed, 3 * l + k // 2 + 1)
                    else:
                        dve.wait_ge(w_used, first_down + N_DN)
                    dve.scalar_tensor_tensor(out=xT[:, k, :], in0=big[:, k // 2, (k % 2) * T:(k % 2 + 1) * T],
                                             scalar=mods[:, l, 40 + k:41 + k], in1=xT[:, k, :], op0=ALU.mult,
                                             op1=ALU.add).then_inc(x_updated, 1)

            out_projection(0, EO)
            ffn(0, UP0, DN0, 1)
            keep_mods(2, 16, aux[:, 1])
            take_mods(2, 1, 0, 16, aux[:, 1])
            make_gain(2, 1, 8, V_NMIX + KT)
            norm(2, mods[:, 1, 0:8], order=lambda a: (a.rearrange("p (r b) -> p b r", r=RES),
                                                      a.rearrange("p (b r) -> p b r", r=RES)))
            dve.wait_ge(acc_zeroed, 3)
            stream(dve, OI, 12, 4, in_step(OI, ADA3, 0, 2))
            stream(dve, OI + 12, 4, 4, in_step(OI + 12, ADA3, 24, 1))
            for n, tile, count in ((16, 28, 2), (17, 30, 2), (18, 32, 0), (19, 32, 0)):
                in_step(OI + n, ADA3, tile, count)(0, OI + n)

            def beside_dilated(s):
                if s == 2:
                    keep_mods(3, 32, acc[:, 1])
                if s in (8, 12):
                    split_lo(0, OO + s // 4 - 2)

            attend(STEPS, cs, ctok, dil_shift, beside_dilated)
            mixed_lo(MIX_AT[1] + 1, 0)
            dve.wait_ge(mod_kept, 4)
            dve.wait_ge(mod_gathered, 5)
            dve.tensor_tensor(mod_rows[:], mod_rows[:], acc[0:32, 1, 0:P], ALU.add).then_inc(mod_kept, 1)
            mixed_lo(MIX_AT[1] + 2, 1)
            take_mods(3, 1, 16, 32, big[:, 3])
            make_gain(3, 1, 32, V_NFFN + KT)
            out_projection(1, OO)
            ffn(1, UP1, DN1, 3)

            reciprocal_rms(4)
            for k in range(KT):
                dve.scalar_tensor_tensor(out=work[:, k, :], in0=xT[:, k, :], scalar=vecs[:, V_FIN + k:V_FIN + k + 1],
                                         in1=rstd[:], op0=ALU.mult, op1=ALU.mult).then_inc(y_ready, 1)
            dve.wait_ge(y_turned, 2)
            dve.tensor_copy(y_tok[:, 1, :], big[:, 2:4, :].rearrange("p b n -> p (b n)")).then_inc(y_copied[1], 1)

        @block.tensor
        def _(pe):
            def three(dst, w, h, start, stop, swap=False):
                for n, (a, b) in enumerate(((w[0], h[0]), (w[0], h[1]), (w[1], h[0]))):
                    lhsT, rhs = (b, a) if swap else (a, b)
                    ins = pe.matmul(dst, lhsT, rhs, start=start and n == 0, stop=stop and n == 2, skip_group_check=True)
                return ins

            def split_ready(i, per, n):
                pe.wait_ge(s_lo, i * (2 * per) + 2 * n + 2)

            def feature_major(n, a, h_from=None, order=range(KT), per=1):
                steps = [(k, g) for k in order for g in (0, 1)] if h_from is not None else \
                    [(k, g) for g in (0, 1) for k in range(KT)]
                for count, (k, g) in enumerate(steps):
                    if h_from is not None and count % (2 * per) == 0:
                        pe.wait_ge(h_lo_ready, h_from + count // (2 * per) + 1)
                    cols = slice(k * 256 + g * P, k * 256 + (g + 1) * P)
                    ins = three(acc[:, a, g * T:(g + 1) * T], (w_hi[:, n % SPLIT, cols], w_lo[:, n % SPLIT, cols]),
                                (h_hi[:, k, :], h_lo[:, k, :]), count == 0 if h_from is not None else k == 0,
                                count >= len(steps) - 2 if h_from is not None else k == KT - 1)
                ins.then_inc(w_used, 1)

            def token_major(n, a, order=None):
                for t in range(TT):
                    for k in range(KT):
                        cols = slice(k * 256, (k + 1) * 256)
                        hk = order(k, t) if order else (h_hi[:, k, t * P:(t + 1) * P], h_lo[:, k, t * P:(t + 1) * P])
                        ins = three(acc[:, a, t * T:(t + 1) * T], (w_hi[:, n % SPLIT, cols], w_lo[:, n % SPLIT, cols]),
                                    hk, k == 0, k == KT - 1, swap=True)
                ins.then_inc(w_used, 1)

            def staggered(k, t):
                return (h_hi[:, k, 64:192], h_lo[:, k, 64:192]) if t == 0 else (wrap_hi[:, k, :], wrap_lo[:, k, :])

            def units(first, start, count, form, freed, freed_base, fresh=2, h_from=None):
                def step(i, n):
                    split_ready(i, 2, n)
                    if not isinstance(i, int) or n - first >= fresh:
                        pe.wait_ge(freed, i * (2 * freed_per) + (freed_base + (n - first) * freed_per - freed_per))
                    form(n, (n - first) % 2, **({"h_from": h_from} if h_from is not None and n == start else {}))
                freed_per = 2 if freed is x_updated else 1
                head = min(count, max(0, first + fresh - start))
                for n in range(start, start + head):
                    step(0, n)
                stream(pe, start + head, count - head, 2, step)

            def norm_sum_of(idx, first=0, last=KT):
                for k in range(first, last):
                    pe.wait_ge(norm_sq, KT * idx + k + 1)
                    ins = pe.matmul(aux[:, 0, 0:T], mean_w, squared[idx][:, k, :], start=(k == 0), stop=(k == KT - 1),
                                    skip_group_check=True)
                if last == KT:
                    ins.then_inc(norm_sum, 1)

            def mod_sum(e, tiles, count, bank, first=0, last=None):
                pe.wait_ge(ada_used, tiles)
                last = count if last is None else last
                for g in range(first, last):
                    pick = consts[:, C_PICK + 31 - g:C_PICK + 31 - g + count]
                    ins = pe.matmul(bank[0:count, 0:P], pick, mod_acc[:, g * P:(g + 1) * P], start=g == first,
                                    stop=g == last - 1)
                ins.then_inc(mod_gathered, 1)

            def mod_turn(e, count, bank):
                pe.wait_ge(mod_kept, e + 1 + (e == 3))
                pe.transpose(bank[:, P:P + count], mod_rows[0:count, :], ident[0:count, 0:count]).then_inc(mod_summed, 1)

            pe.wait_ge(s_ident, 16)
            pe.wait_ge(s_rows, 16 * 11)
            pe.transpose(aux[:, 0, 0:104], rows_a[:], ident[0:104, 0:104])
            pe.transpose(aux[:, 0, 104:197], rows_b[:], ident[0:93, 0:93])
            for l in (0, 1):
                at0 = V_CW + l * 3 * FT
                ins = pe.transpose(aux[:, 0, at0:at0 + 3 * FT], rows_c[:, l, :], ident[0:3 * FT, 0:3 * FT])
            ins.then_inc(rows_turned, 1)
            pe.wait_ge(s_x, 16)
            for b in range(4):
                for k in (2 * b, 2 * b + 1):
                    for t in range(TT):
                        to = (k % 2) * T + t * P
                        ins = pe.transpose(big[:, b, to:to + P], x_tok[:, t, k * P:(k + 1) * P], ident)
                ins.then_inc(x_turned, 1)
            norm_sum_of(0)
            mod_sum(0, ADA1, 16, aux[:, 1])
            mod_turn(0, 16, aux[:, 1])

            units(EI, EI, 6, feature_major, z_evicted, 0, h_from=NORM_AT[0])
            units(EI, EI + 6, 2, token_major, z_evicted, 0)

            def turn_bias(first, last):
                for b in range(first, last):
                    if b >= 4:
                        pe.wait_ge(bias_kept, b - 3)
                    pe.matmul(big[:, b % 4, :], consts[:, C_FLIP:C_FLIP + P],
                              nflip[:].rearrange("p h e c -> p (h e c)")[:, b * 512:(b + 1) * 512], start=True,
                              stop=True).then_inc(bias_turned, 1)

            units(EI, EI + 8, 2, feature_major, z_evicted, 0)
            pe.wait_ge(s_const, 16)
            pe.wait_ge(s_bias, 16 * 2 * NA_HEADS)
            turn_bias(0, 4)
            units(EI, EI + 10, 2, feature_major, z_evicted, 0)
            turn_bias(4, 6)
            units(EI, EI + 12, 2, feature_major, z_evicted, 0)
            units(EI, EI + 14, 2, token_major, z_evicted, 0)

            def attend(base, width, scores_of, values_of, kept, tok, values_at, beside=lambda s: None):
                for s in range(STEPS + 6):
                    if s < STEPS:
                        if s >= 3:
                            pe.wait_ge(shifted, base + s - 2)
                        scores_of(big[:, s % 3, :], 2 * (s // 4) + s % 2, s // 2 % 2).then_inc(scored, 1)
                    beside(s)
                    if 0 <= s - 2 < STEPS:
                        r = s - 2
                        pe.wait_ge(exp_done, base + r + 1)
                        if r >= 2:
                            pe.wait_ge(probs_kept, base + r - 1)
                        for j in range(width // P):
                            ins = pe.transpose(aux[:, r % 2, j * P:(j + 1) * P],
                                               (ns if base == 0 else cs)[:, r % 4, j * P:(j + 1) * P], ident)
                        ins.then_inc(turned, 1)
                    if 0 <= s - 3 < STEPS:
                        r = s - 3
                        if r == 0:
                            pe.wait_ge(z_evicted, values_at)
                        pe.wait_ge(probs_kept, base + r + 1)
                        if r >= 2:
                            pe.wait_ge(out_taken, base + r - 1)
                        values_of(acc[:, r % 2, 0:DH], kept[:, r % 2, :], 2 * (r // 4) + r % 2,
                                  r // 2 % 2).then_inc(attended, 1)
                    if s >= 6 and s % 2 == 0:
                        j = (s - 6) // 2
                        pe.wait_ge(out_taken, base + 2 * j + 2)
                        if j >= 1:
                            pe.wait_ge(out_placed, base // 2 + j)
                        pe.transpose(big[:, 3, 0:P], tok[:, j % 2, :], ident).then_inc(out_turned, 1)

            def nat_scores(bank, h, t):
                lane = slice((h % 2) * DH, (h % 2 + 1) * DH)
                cols = (h // 2 % 2) * T
                q = ze[lane, 10 + h // 4, cols + t * P:cols + (t + 1) * P]
                return pe.matmul(bank[:, 0:T], q, ze[lane, 12 + h // 4, cols:cols + T], start=True, stop=True)

            def nat_values(dst, probs, h, t):
                for kt in range(TT):
                    v = ze[:, 14 + h // 4, kt * T + (h % 4) * DH:kt * T + (h % 4 + 1) * DH]
                    ins = pe.matmul(dst, probs[:, kt * P:(kt + 1) * P], v, start=(kt == 0), stop=(kt == TT - 1))
                return ins

            pe.wait_ge(z_evicted, 14)
            attend(0, T, nat_scores, nat_values, npt, ntok, N_EI)

            for s, (d, h) in enumerate(GLA_STEPS):
                level = 0 if h == 0 else LEVELS.index(h)
                pe.wait_ge(gla_ready[d], 1 if h == 0 else level + 1 + (d == 0))
                queries = qT if h == 0 else gq_l[level % 2][:, d, :]
                keys = gk[:, d, :] if h == 1 else gk_l[level % 2][:, d, :]
                if h < SB:
                    n = SMALL.index(s)
                    if n >= 4:
                        pe.wait_ge(diag_taken, n - 3)
                    for hd in range(A_HEADS):
                        for b in range(T // SB):
                            toks = slice(hd * T + b * SB, hd * T + (b + 1) * SB)
                            row, col = (b % 2) * SB, (hd * TT + b // 2) * SB
                            ins = pe.matmul(diag_banks[n % 4][row:row + SB, col:col + SB], keys[:, toks], queries[:, toks],
                                            start=True, stop=True, skip_group_check=True)
                else:
                    for hd in range(A_HEADS):
                        for b in range(T // (2 * h)):
                            left, right = 2 * h * b, 2 * h * b + h
                            ktok, qtok = (left, right) if d == 0 else (right, left)
                            row, t = ktok % P, ktok // P
                            ins = pe.matmul(big[row:row + h, hd, t * T + qtok:t * T + qtok + h],
                                            keys[:, hd * T + ktok:hd * T + ktok + h],
                                            queries[:, hd * T + qtok:hd * T + qtok + h], start=True, stop=True,
                                            skip_group_check=True)
                ins.then_inc(gla_done, 1)
            pe.wait_ge(att_copied, 2)
            pe.wait_ge(att_ready, 1)
            for b in (0, 1):
                for hd in (2 * b, 2 * b + 1):
                    for t in range(TT):
                        v = ze[:, 6 + hd // 2, t * T + (hd % 2) * P:t * T + (hd % 2 + 1) * P]
                        ins = pe.matmul(acc[:, b, (hd % 2) * T:(hd % 2 + 1) * T], v, att[:, hd, t, :], start=(t == 0),
                                        stop=(t == TT - 1))
                ins.then_inc(gla_out, 1)
            for b in (0, 1):
                pe.wait_ge(gla_sq, 2 * b + 2)
                pe.matmul(aux[:, b, :], hmean_w, gq_l[1][:, 0, b * 512:(b + 1) * 512], start=True, stop=True).then_inc(
                    gla_mean, 1)
            mod_sum(1, ADA2, 32, big[:, 0])
            mod_turn(1, 32, big[:, 0])

            def ffn(l, first_up, first_down, idx):
                norm_sum_of(idx, 6)
                units(first_up, first_up, N_UP, feature_major, hid_ready, l * FT, h_from=NORM_AT[idx])
                def down_unit(i, n):
                    split_ready(i, 2, n)
                    u = n - first_down
                    pe.wait_ge(hid_lo_ready, i * 4 + (l * FT + 2 * u + 2))
                    last = isinstance(i, int) and u == N_DN - 1
                    order = [(kk, g) for g in range(KT) for kk in (0, 1)] if last else \
                        [(kk, g) for kk in (0, 1) for g in range(KT)]
                    for kk, g in order:
                            hk = bass.ds(i * 4 + (2 * u + kk), 1)
                            hh = [a[:, hk, :].rearrange("p u n -> p (u n)") for a in (hid_hi, hid_lo)]
                            cols = slice(kk * D + g * P, kk * D + (g + 1) * P)
                            ins = three(big[:, g // 2, (g % 2) * T:(g % 2 + 1) * T],
                                        (w_hi[:, n % SPLIT, cols], w_lo[:, n % SPLIT, cols]), hh,
                                        isinstance(i, int) and u == 0 and kk == 0 and g % 2 == 0,
                                        last and kk == 1)
                            if last and g % 2 and kk and g < KT - 1:
                                ins.then_inc(down_summed, 1)
                    ins.then_inc(w_used, 1)
                down_unit(0, first_down)
                stream(pe, first_down + 1, N_DN - 3, 2, down_unit)
                for n in range(first_down + N_DN - 2, first_down + N_DN):
                    down_unit(0, n)

            halves_at = lambda value, order: lambda n, a: feature_major(n, a, value, order, KT // 2)
            for u in range(N_EO):
                form = halves_at(MIX_AT[0], (4, 5, 6, 7, 0, 1, 2, 3)) if u == 0 else feature_major
                units(EO, EO + u, 1, form, x_updated, 0)
                if u >= 1:
                    norm_sum_of(1, 2 * u - 2, 2 * u)
            ffn(0, UP0, DN0, 1)
            mod_sum(2, ADA3, 16, aux[:, 1])
            norm_sum_of(2)
            mod_turn(2, 16, aux[:, 1])
            units(OI, OI, 12, feature_major, z_evicted, N_EI, h_from=NORM_AT[2])
            units(OI, OI + 12, 4, token_major, z_evicted, N_EI)
            pe.wait_ge(wrapped, 4)
            units(OI, OI + 16, 2, lambda n, a: token_major(n, a, staggered), z_evicted, N_EI)
            units(OI, OI + 18, 2, feature_major, z_evicted, N_EI)
            def dil_scores(bank, h, t):
                lane = slice((h % 2) * DH, (h % 2 + 1) * DH)

                def rows(first, g, tok0, tokens):
                    f = g * 4 + h // 2
                    return zo[lane, first + f // 2, (f % 2) * T + tok0:(f % 2) * T + tok0 + tokens]
                pe.matmul(bank[:, 0:T], rows(0, 0, t * P, P), rows(6, 0, 0, T), start=True, stop=True)
                for side in (0, 1):
                    tok0 = t * P + 64 * side
                    for block, g in enumerate((1, 2) if side == 0 else (2, 1)):
                        at0 = T + 64 * block
                        ins = pe.matmul(bank[64 * side:64 * side + 64, at0:at0 + 64], rows(0, g, tok0, 64),
                                        rows(6, g, tok0, 64), start=True, stop=True, skip_group_check=True)
                return ins

            def dil_values(dst, probs, h, t):
                for kt in range(TT):
                    v = zo[:, 12 + h // 4, kt * T + (h % 4) * DH:kt * T + (h % 4 + 1) * DH]
                    pe.matmul(dst, probs[:, kt * P:(kt + 1) * P], v, start=(kt == 0), stop=False, skip_group_check=True)
                for side in (0, 1):
                    v = zo[:, 14 + 2 * t + side, h * DH:(h + 1) * DH]
                    ins = pe.matmul(dst[64 * side:64 * side + 64, :], probs[:, T + 64 * side:T + 64 * side + 64], v,
                                    start=False, stop=True, skip_group_check=True)
                return ins

            def half_mods(s):
                if s == 2:
                    pe.wait_ge(z_evicted, N_EI + N_OI)
                    mod_sum(3, ADAS, 32, acc[:, 1], 0, 16)
                if s == 4:
                    pe.wait_ge(mod_kept, 4)

            attend(STEPS, ROW, dil_scores, dil_values, cpt, ctok, N_EI + N_OI, half_mods)

            pe.wait_ge(s_poolw, 16)
            pe.wait_ge(pool_step, POOL_STEPS)
            for g in range(4):
                ins = pe.matmul(big[:, g // 2, (g % 2) * T:(g % 2 + 1) * T], poolw[:, g, :], pmean[:, g, :], start=True,
                                stop=True)
            ins.then_inc(pool_mixed, 1)
            mod_sum(3, ADAS, 32, acc[:, 1], 16, 32)

            for u in range(N_OO):
                form = halves_at(MIX_AT[1], range(KT)) if u == 0 else feature_major
                units(OO, OO + u, 1, form, x_updated, 16)
                if u == 0:
                    mod_turn(3, 32, big[:, 3])
                if u >= 1:
                    norm_sum_of(3, 2 * u - 2, 2 * u)
            ffn(1, UP1, DN1, 3)
            norm_sum_of(4)
            for t in range(TT):
                for k in range(KT):
                    if t == 0:
                        pe.wait_ge(y_ready, k + 1)
                    ins = pe.transpose(big[:, 2 * t + k // 4, (k % 4) * P:(k % 4 + 1) * P],
                                       work[:, k, t * P:(t + 1) * P], ident)
                ins.then_inc(y_turned, 1)



_INS = ("x", "c", "ada_w", "ada_b", "norm_mix_g", "norm_ffn_g", "even_w_in", "even_w_out", "hgrn_lb_logits",
        "hgrn_norm_g", "na_rpb", "odd_w_in", "odd_w_out", "pool_w", "pool_scale", "ffn_w_up", "ffn_conv_w",
        "ffn_conv_b", "ffn_w_down", "final_norm_g")


def kernel(**inputs):
    import concourse.bacc as bacc
    from concourse.bass_utils import run_bass_kernel_spmd

    nc = bacc.Bacc("TRN2", target_bir_lowering=False, num_devices=1)
    arrays = {f"in_{name}": np.ascontiguousarray(inputs[name]) for name in _INS}
    arrays["in_shape_constants"] = shape_constants()
    args = [nc.dram_tensor(name, a.shape, mybir.dt.from_np(a.dtype), kind="ExternalInput").ap()
            for name, a in arrays.items()]
    out = nc.dram_tensor("out", (1, T, D), F32, kind="ExternalOutput").ap()
    encoder(nc, *args, out)
    r = run_bass_kernel_spmd(nc, [arrays], core_ids=[0])
    return r.results[0]["out"]
```

```python
from contextlib import ExitStack

import numpy as np

import concourse.bass as bass
from concourse import mybir

ALU = mybir.AluOpType
ACT = mybir.ActivationFunctionType
AX_X = mybir.AxisListType.X
F32 = mybir.dt.float32
F32R = mybir.dt.float32r
I32 = mybir.dt.int32

P = 128
D = 1024
T = 256
KT = D // P
TT = T // P
EPS = 1e-6
LB_FLOOR = 1e-12
BIG = 1e30
D_FF = 2816
FT = D_FF // P
GRID_W, NA_KR, NA_KC = 64, 8, 16
NA_HEADS, DH = 8, 64
A_HEADS = 4
C_GROUPS, C_HEADS = 3, 8
C_CONFIGS = ((128, 1), (512, 4), (2048, 16))
WINDOWS = (2, 4, 8, 16)
SCALE = DH ** -0.5

UNIT = 2048
RAW = 4
SPLIT = 2
EI, EO, UP0, DN0, OI, OO, UP1, DN1, UNITS = (0, 16, 20, 42, 53, 73, 77, 99, 110)
N_EI, N_EO, N_UP, N_DN, N_OI, N_OO = 16, 4, FT, FT // 2, 20, 4
ADA1, ADA2, ADA3, ADAS = 8, 40, 56, 88

LEVELS = (1, 2, 4, 8, 16, 32, 64, 128)
GLA_STEPS = 1 + len(LEVELS)
SB = 64
SMALL = 1 + LEVELS.index(SB)
STEPS = 16
RES = 4
ROW = T + 2 * T // RES

C_ID, C_MEAN, C_EPS = 0, 128, 256
C_PICK = C_EPS + 1
C_HMEAN = C_PICK + 63
C_NAT = C_HMEAN + P
C_LVL = C_NAT + GRID_W
C_FLIP = C_LVL + (SMALL - 1) * SB
C_DIST = C_FLIP + P
C_SLOPE = C_DIST + TT * ROW
C_INV = C_SLOPE + 2 * C_HEADS
C_ALL = C_INV + 4 * T

V_C, V_ADAB = 0, 8
V_NMIX, V_NFFN, V_FIN, V_PSC, V_LB, V_HG, V_CB = 104, 120, 136, 144, 148, 152, 153
V_CW = 197
V_ALL = V_CW + 2 * 3 * FT


NORM_AT = (0, 10, 18, 28)
MIX_AT = (8, 26)


def slope(g, h):
    return 2.0 ** (-8.0 * (g * C_HEADS + h + 1) / (C_GROUPS * C_HEADS))


def shape_constants():
    a = np.zeros((P, C_ALL), np.float32)
    p = np.arange(P)
    a[:, C_ID:C_ID + P] = np.eye(P)
    a[:, C_MEAN:C_MEAN + P] = 1.0 / D
    a[:, C_HMEAN:C_HMEAN + P] = 1.0 / P
    key = np.arange(T)
    half, b = p // 64, p % 64
    for t in range(TT):
        query = RES * b + 2 * t + half
        keys = np.concatenate([np.tile(RES * (key % 64) + key // 64, (P, 1)),
                               np.tile(RES * np.arange(64), (P, 2)) + (2 * t + half)[:, None]], 1)
        group = np.concatenate([np.zeros((P, T), int), np.repeat(np.where(half, 2, 1)[:, None], 64, 1),
                                np.repeat(np.where(half, 1, 2)[:, None], 64, 1)], 1)
        off = np.abs(keys - query[:, None])
        window = np.array([w for w, _ in C_CONFIGS])[group]
        dil = np.array([d for _, d in C_CONFIGS])[group]
        ok = (off % dil == 0) & (off <= window // 2 // dil * dil)
        a[:, C_DIST + t * ROW:C_DIST + (t + 1) * ROW] = np.where(ok, off, BIG)
    for h in range(C_HEADS):
        a[:, C_SLOPE + 2 * h] = np.where(half, -slope(2, h), -slope(1, h))
        a[:, C_SLOPE + 2 * h + 1] = np.where(half, -slope(1, h), -slope(2, h))
    c, kc = (p % GRID_W)[:, None], np.arange(GRID_W)[None, :]
    first = np.clip(c - NA_KC // 2, 0, GRID_W - NA_KC)
    a[:, C_NAT:C_NAT + GRID_W] = np.where((kc >= first) & (kc < first + NA_KC), 0.0, -BIG)
    s, q = (p % SB)[:, None], np.arange(SB)[None, :]
    for n, h in enumerate(LEVELS[:SMALL - 1]):
        a[:, C_LVL + n * SB:C_LVL + (n + 1) * SB] = (s // (2 * h) == q // (2 * h)) & (s // h != q // h)
    for g, w in enumerate(WINDOWS):
        lo, hi = np.clip(key - w // 2, 0, T), np.clip(key + w - w // 2, 0, T)
        a[:, C_INV + g * T:C_INV + (g + 1) * T] = 1.0 / (hi - lo).astype(np.float32)
    a[:, C_EPS] = EPS
    a[:, C_PICK + 31] = 1.0
    a[:, C_FLIP:C_FLIP + P] = (p[:, None] // GRID_W == p[None, :] // GRID_W) & \
        (p[:, None] % GRID_W + p[None, :] % GRID_W == GRID_W - 1)
    return a


def encoder(nc, x, c, ada_w, ada_b, norm_mix_g, norm_ffn_g, even_w_in, even_w_out, hgrn_lb_logits, hgrn_norm_g,
            na_rpb, odd_w_in, odd_w_out, pool_w, pool_scale, ffn_w_up, ffn_conv_w, ffn_conv_b, ffn_w_down,
            final_norm_g, consts_in, out):
    with ExitStack() as ctx:
        place = [(nc.sbuf_base + 63) // 64 * 64]

        def at(name, shape, dt, offset):
            return nc.alloc_sbuf_tensor_at(name, shape, dt, offset=offset)

        def sb(name, shape, dt=F32):
            n = 4
            for s in shape[1:]:
                n *= s
            t = at(name, shape, dt, place[0])
            place[0] += (n + 63) // 64 * 64
            return t

        def sem(name):
            return ctx.enter_context(nc.semaphore(name))

        w_raw = sb("w_raw", [P, RAW, UNIT])
        w_hi = sb("w_hi", [P, SPLIT, UNIT], F32R)
        w_lo = sb("w_lo", [P, SPLIT, UNIT], F32R)
        ada_raw = sb("ada_raw", [P, 2, 1024])
        mod_acc = sb("mod_acc", [P, 4096])
        xT = sb("xT", [P, KT, T])
        h_at = place[0]
        h_hi = sb("h_hi", [P, KT, T], F32R)
        h_lo = sb("h_lo", [P, KT, T], F32R)
        work = sb("work", [P, KT, T])
        consts = sb("consts", [P, C_ALL])
        vecs = sb("vecs", [P, V_ALL])
        cact = sb("cact", [P, KT])
        mods = sb("mods", [P, 2, 48])
        gain = sb("gain", [P, 4, KT])
        rstd = sb("rstd", [P, T])
        lbt = sb("lbt", [P, 6, A_HEADS])
        mod_rows = sb("mod_rows", [32, P])
        table_sink = sb("table_sink", [P, 1])
        stat = sb("stat", [P, 4, 4])
        poolw = sb("poolw", [P, 4, P])
        arena = place[0]
        assert arena + 69 * 1024 <= nc.sbuf_usable_end, (arena, nc.sbuf_usable_end)

        K = 1024
        squared = [at(f"squared{n}", [P, KT, T], F32, arena + first * K) for n, first in enumerate((40, 60, 60, 60, 60))]
        ada_first = [at(f"ada_first{k}", [P, 2048], F32, arena + 8 * k * K)[:] for k in range(5)]
        ada_first += [ada_raw[:].rearrange("p s n -> p (s n)"), mod_acc[:, 2048:4096],
                      work[:].rearrange("p k t -> p (k t)")]
        x_tok = at("x_tok", [P, TT, D], F32, arena + 40 * K)
        rows_a = at("rows_a", [104, P], F32, arena + 48 * K)
        rows_b = at("rows_b", [93, P], F32, arena + 49 * K)
        rows_c = at("rows_c", [3 * FT, 2, P], F32, arena + 50 * K)
        nflip = at("nflip", [P, NA_HEADS, 6, GRID_W], F32, arena + 56 * K)
        ze = at("ze", [P, N_EI, 512], F32, arena)
        nbias = at("nbias", [P, NA_HEADS, 6, GRID_W], F32, arena + 32 * K)
        ns = at("ns", [P, 4, T], F32, arena + 44 * K)
        npt = at("npt", [P, 2, TT * P], F32, arena + 48 * K)
        ntok = at("ntok", [P, 2, P], F32, arena + 50 * K)
        diag = at("diag", [P, A_HEADS * TT, SB], F32, arena + 20 * K)
        gk = at("gk", [P, 2, A_HEADS * T], F32, arena + 60 * K)
        att = at("att", [P, A_HEADS, TT, T], F32, arena + 32 * K)
        gex = [at("gex0", [P, A_HEADS * T], F32, arena + 56 * K)[:], at("gex1", [P, A_HEADS * T], F32, h_at + 12 * K)[:]]
        gq_l = [at(f"gq_l{n}", [P, A_HEADS * T], F32, a)[:] for n, a in enumerate((h_at, arena + 44 * K))]
        gk_l = [at(f"gk_l{n}", [P, A_HEADS * T], F32, a)[:] for n, a in enumerate((h_at + 8 * K, arena + 52 * K))]
        gk_own = at("gk_own", [P, A_HEADS * T], F32, h_at + 4 * K)[:]
        hid_hi = at("hid_hi", [P, FT, T], F32R, arena)
        hid_lo = at("hid_lo", [P, FT, T], F32R, arena + 22 * K)
        conv = at("conv", [P, 2, T], F32, arena + 44 * K)
        gated = at("gated", [P, 2, T], F32, arena + 46 * K)
        hid = at("hid", [P, 2, T], F32, arena + 48 * K)
        zo = at("zo", [P, N_OI, 512], F32, arena)
        wrap_hi = at("wrap_hi", [P, KT, 2 * 64], F32R, arena + 40 * K)
        wrap_lo = at("wrap_lo", [P, KT, 2 * 64], F32R, arena + 44 * K)
        cs = at("cs", [P, 4, ROW], F32, arena + 40 * K)
        cpt = at("cpt", [P, 2, ROW], F32, arena + 46 * K)
        ctok = at("ctok", [P, 2, P], F32, arena + 49 * K)
        PADW = T + 16
        pu = at("pu", [P, 4, PADW], F32, arena + 52 * K)
        pw = [at(f"pw{w}", [P, 4, PADW], F32, arena + 52 * K + (n + 1) * 4352) for n, w in enumerate((2, 4, 8))]
        pmean = at("pmean", [P, 4, T], F32, arena + 52 * K)
        y_tok = at("y_tok", [P, TT, D], F32, arena + 52 * K)

        acc = ctx.enter_context(nc.psum_tensor("acc", [P, 2, 512], F32))
        big = ctx.enter_context(nc.psum_tensor("big", [P, 4, 512], F32))
        aux = ctx.enter_context(nc.psum_tensor("aux", [P, 2, 512], F32))

        diag_banks = [aux[:, 0], aux[:, 1], acc[:, 0], acc[:, 1]]
        ident = consts[:, C_ID:C_ID + P]
        mean_w = consts[:, C_MEAN:C_MEAN + P]
        hmean_w = consts[:, C_HMEAN:C_HMEAN + P]
        qT = ze[:, 0:2, :].rearrange("p u n -> p (u n)")
        fT = [ze[:, 2:4, :].rearrange("p u n -> p (u n)"), ze[:, 4:6, :].rearrange("p u n -> p (u n)")]
        gT = ze[:, 8:10, :].rearrange("p u n -> p (u n)")

        s_ident, s_const, s_x, s_rows = sem("s_ident"), sem("s_const"), sem("s_x"), sem("s_rows")
        bias_turned, bias_kept = sem("bias_turned"), sem("bias_kept")
        s_bias, s_odd, s_out = sem("s_bias"), sem("s_odd"), sem("s_out")
        first_landed = [sem(f"first_landed{k}") for k in range(KT)]
        w_landed = [sem(f"w_landed{i}") for i in range(RAW)]
        s_hi, s_lo, w_used = sem("s_hi"), sem("s_lo"), sem("w_used")
        ada_landed = [sem(f"ada_landed{i}") for i in range(2)]
        rest_landed = [sem(f"rest_landed{i}") for i in range(2)]
        ada_used, acc_zeroed, mod_summed, mod_ready = sem("ada_used"), sem("acc_zeroed"), sem("mod_summed"), sem("mod_ready")
        rows_turned, vecs_ready, x_turned, x_ready, cact_ready = (
            sem("rows_turned"), sem("vecs_ready"), sem("x_turned"), sem("x_ready"), sem("cact_ready"))
        gain_ready, norm_sq, norm_sum, rstd_ready, norm_mul, h_hi_ready, h_lo_ready = (
            sem("gain_ready"), sem("norm_sq"), sem("norm_sum"), sem("rstd_ready"), sem("norm_mul"), sem("h_hi_ready"),
            sem("h_lo_ready"))
        rms_ready, gla_rms = sem("rms_ready"), sem("gla_rms")
        z_evicted, x_updated, dve_chain = sem("z_evicted"), sem("x_updated"), sem("dve_chain")
        conv_mid, conv_taps, silu_ready, hid_ready, hid_hi_ready, hid_lo_ready = (
            sem("conv_mid"), sem("conv_taps"), sem("silu_ready"), sem("hid_ready"), sem("hid_hi_ready"),
            sem("hid_lo_ready"))
        scored, shifted, exp_done, turned, probs_kept, attended, out_taken, out_turned, out_placed = (
            sem("scored"), sem("shifted"), sem("exp_done"), sem("turned"), sem("probs_kept"), sem("attended"),
            sem("out_taken"), sem("out_turned"), sem("out_placed"))
        wrapped = sem("wrapped")
        lb_diff, lb_exp, lb_ready, gate_act, gates_ready, gla_done, diag_taken, att_copied, att_ready = (
            sem("lb_diff"), sem("lb_exp"), sem("lb_ready"), sem("gate_act"), sem("gates_ready"),
            sem("gla_done"), sem("diag_taken"),
            sem("att_copied"), sem("att_ready"))
        gla_out, gla_sq, gla_mean, gla_normed, gla_cleared = (
            sem("gla_out"), sem("gla_sq"), sem("gla_mean"), sem("gla_normed"), sem("gla_cleared"))
        ahead_grown, own_ready = sem("ahead_grown"), sem("own_ready")
        gla_ready = [sem("gla_ready_back"), sem("gla_ready_ahead")]
        down_summed, mod_gathered, mod_kept = sem("down_summed"), sem("mod_gathered"), sem("mod_kept")
        pool_step, pool_mixed, pool_taken = sem("pool_step"), sem("pool_mixed"), sem("pool_taken")
        y_ready, y_turned, y_copied = sem("y_ready"), sem("y_turned"), [sem(f"y_copied{t}") for t in range(TT)]

        def stream(eng, first, count, unroll, step):
            trips = count // unroll
            if trips > 1:
                with eng.Fori(0, trips) as i:
                    for j in range(unroll):
                        step(i, first + j)
            elif trips == 1:
                for j in range(unroll):
                    step(0, first + j)
            for j in range(trips * unroll, count):
                step(0, first + j)

        def half_of(a, h, side):
            return a.rearrange("p (b two h) -> p b two h", two=2, h=h)[:, :, side, :]

        def take_part(eng, to, frm, factor, h, side):
            return eng.tensor_tensor(half_of(to, h, side), half_of(frm, h, side), half_of(factor, h, side), ALU.mult)

        def grow(eng, to, d, h, side):
            edge = h - 1 if d == 0 else 0
            total = half_of(fT[d], h, 1 - side)[:, :, edge:edge + 1].to_broadcast([P, A_HEADS * T // (2 * h), h])
            return eng.tensor_tensor(half_of(to, h, side), half_of(to, h, side), total, ALU.mult)

        block = ctx.enter_context(nc.Block())

        @block.sync
        def _(sp):
            sp.dma_start(consts[:, :C_HMEAN], consts_in[:, :C_HMEAN]).then_inc(s_ident, 16)
            sp.dma_start(x_tok[:], x.rearrange("b (t p) d -> p (b t) d", p=P)).then_inc(s_x, 16)
            sp.dma_start(ada_first[0], ada_w[0, 0:P, 0:2048]).then_inc(first_landed[0], 16)
            sp.dma_start(rows_a[0:8, :], c.rearrange("o (k p) -> (o k) p", p=P)).then_inc(s_rows, 16)
            sp.dma_start(rows_a[8:104, :], ada_b.rearrange("l (k p) -> (l k) p", p=P)).then_inc(s_rows, 16)
            sp.dma_start(rows_b[0:16, :], norm_mix_g.rearrange("l (k p) -> (l k) p", p=P)).then_inc(s_rows, 16)
            sp.dma_start(rows_b[16:32, :], norm_ffn_g.rearrange("l (k p) -> (l k) p", p=P)).then_inc(s_rows, 16)
            sp.dma_start(rows_b[32:40, :], final_norm_g.rearrange("(k p) -> k p", p=P)).then_inc(s_rows, 16)
            sp.dma_start(rows_b[40:44, :], pool_scale.rearrange("o (k p) -> (o k) p", p=P)).then_inc(s_rows, 16)
            sp.dma_start(rows_b[44:48, :], hgrn_lb_logits.rearrange("o (k p) -> (o k) p", p=P)).then_inc(s_rows, 16)
            sp.dma_start(rows_b[48:49, :], hgrn_norm_g).then_inc(s_rows, 16)
            sp.dma_start(rows_b[49:93, :], ffn_conv_b.rearrange("l (k p) -> (l k) p", p=P)).then_inc(s_rows, 16)
            for l in (0, 1):
                sp.dma_start(rows_c[:, l, :], ffn_conv_w[l].rearrange("j (k p) -> (j k) p", p=P)).then_inc(s_rows, 16)
            for k in range(1, KT):
                sp.dma_start(ada_first[k], ada_w[0, k * P:(k + 1) * P, 0:2048]).then_inc(first_landed[k], 16)
            def load(i, n, src, halves_of="k"):
                if not (isinstance(i, int) and 4 * i + n < RAW):
                    sp.wait_ge(s_lo, i * 8 + 2 * (n - RAW + 1))
                slot = n % RAW
                if halves_of == "k":
                    k = src.shape[1]
                    dst = w_raw[:, slot, :].rearrange("p (k n) -> p k n", k=k)
                    for part in (slice(0, k // 2), slice(k // 2, k)):
                        sp.dma_start(dst[:, part, :], src[:, part, :]).then_inc(w_landed[slot], 16)
                else:
                    dst = w_raw[:, slot, :].rearrange("p (k h n) -> p k h n", k=KT, h=2)
                    for h in (0, 1):
                        sp.dma_start(dst[:, :, h, :], src[:, :, h, :]).then_inc(w_landed[slot], 16)

            def columns(w):
                return w.rearrange("(k p) n -> p k n", p=P)

            def project(w, first, count, skip=0):
                stream(sp, first + skip, count - skip, 4,
                       lambda i, n: load(i, n, columns(w)[:, :, bass.ds(i * 1024 + (n - first) * 256, 256)]))

            def up(l, first):
                w = ffn_w_up[l].rearrange("(k p) (h n) -> p k h n", p=P, h=2)
                stream(sp, first, N_UP, 4,
                       lambda i, n: load(i, n, w[:, :, :, bass.ds(i * 512 + (n - first) * P, P)], "h"))

            def down(l, first):
                w = ffn_w_down[l].rearrange("(u k p) n -> u p k n", p=P, k=2)
                stream(sp, first, N_DN, 4, lambda i, n: load(i, n, w[bass.ds(i * 4 + (n - first), 1)]
                                                             .rearrange("u p k n -> p (u k) n")))

            project(even_w_in[0], EI, 4)
            project(even_w_in[0], EI, 6, skip=4)
            sp.dma_start(consts[:, C_HMEAN:C_DIST], consts_in[:, C_HMEAN:C_DIST]).then_inc(s_const, 16)
            rpb_rows = 2 * NA_KC - 1
            for rr in (0, 1):
                first = (NA_KR - 1 - 2 - rr) * rpb_rows + NA_KC - 1 - (GRID_W - 1)
                for h in range(NA_HEADS):
                    src = bass.AP(na_rpb.tensor, na_rpb.offset + first + h * (2 * NA_KR - 1) * rpb_rows,
                                  [[1, GRID_W], [rpb_rows, 6], [1, GRID_W]])
                    sp.dma_start(nflip[rr * GRID_W:(rr + 1) * GRID_W, h], src).then_inc(s_bias, 16)
                project(even_w_in[0], EI, 7 + rr, skip=6 + rr)
            project(even_w_in[0], EI, N_EI, skip=8)
            project(even_w_out[0], EO, N_EO)
            for tile in range(20, 32):
                sp.wait_ge(ada_used, ADA1 + tile - 1)
                k, q, slot = tile // 4, tile % 4, tile % 2
                sp.dma_start(ada_raw[:, slot, :], ada_w[0, k * P:(k + 1) * P, 2048 + q * 1024:3072 + q * 1024]).then_inc(
                    rest_landed[slot], 16)
            sp.dma_start(consts[:, C_DIST:], consts_in[:, C_DIST:]).then_inc(s_odd, 16)
            sp.dma_start(poolw[:], pool_w[0].rearrange("g c d -> c g d")).then_inc(s_odd, 16)
            up(0, UP0)
            down(0, DN0)
            project(odd_w_in[0], OI, N_OI)
            project(odd_w_out[0], OO, N_OO)
            for tile in range(24, 32):
                sp.wait_ge(ada_used, ADA3 + tile - 1)
                k, q, slot = (tile - 16) // 2, 2 + tile % 2, tile % 2
                sp.dma_start(ada_raw[:, slot, :], ada_w[1, k * P:(k + 1) * P, 2048 + q * 1024:3072 + q * 1024]).then_inc(
                    rest_landed[slot], 16)
            up(1, UP1)
            down(1, DN1)
            for t in range(TT):
                sp.wait_ge(y_copied[t], 2)
                sp.dma_start(out[0, t * P:(t + 1) * P, :], y_tok[:, t, :]).then_inc(s_out, 16)
            sp.wait_ge(s_out, 16 * TT)

        @block.gpsimd
        def _(pool):
            def tile_in(l, k, q, slot, i2, t2):
                pool.wait_ge(ada_used, i2 * 2 + 2 * t2 + slot - 1)
                src = ada_w[l].rearrange("(k p) n -> k p n", p=P)[bass.ds(k, 1), :, q:q + 1024]
                pool.dma_start(ada_raw[:, slot, :], src.rearrange("k p n -> p (k n)")).then_inc(ada_landed[slot], 16)

            def head(l, base):
                tile_in(l, 0, 0, 0, 0, base // 2)
                tile_in(l, 0, 1024, 1, 0, base // 2)
                with pool.Fori(1, KT) as k:
                    for q in (0, 1):
                        tile_in(l, k, q * 1024, q, k, base // 2)

            def rest(l, base, first=0, last=KT):
                with pool.Fori(first, last) as k:
                    for q in range(4):
                        tile_in(l, k, 2048 + q * 1024, q % 2, k * 2, base // 2 + q // 2)

            done = [0]

            def link(ins):
                done[0] += 1
                ins.then_inc(pool_step, 1)
                pool.wait_ge(pool_step, done[0])

            pool.wait_ge(mod_gathered, 1)
            pool.memset(mod_acc[:], 0.0).then_inc(acc_zeroed, 1)
            rest(0, ADA1, 0, 5)
            pool.wait_ge(lb_ready, 1)
            pool.wait_ge(gate_act, 4)
            for d in (0, 1):
                for h in range(A_HEADS):
                    cols = slice(h * T, (h + 1) * T)
                    pool.tensor_scalar(fT[d][:, cols], fT[d][:, cols], lbt[:, 5, h:h + 1], lbt[:, 4, h:h + 1],
                                       ALU.mult, ALU.add)
                    ins = pool.tensor_scalar(gk[:, d, cols], gk[:, d, cols], lbt[:, 5, h:h + 1], None, ALU.mult)
            ins.then_inc(gates_ready, 1)
            pool.wait_ge(z_evicted, N_EI)
            pool.wait_ge(gates_ready, 1)
            pool.tensor_tensor(gk_own, gk[:, 0, :], gk[:, 1, :], ALU.add).then_inc(own_ready, 1)
            for exc in gex:
                pool.memset(exc, 1.0).then_inc(gla_cleared, 1)
            pool.wait_ge(gla_cleared, 2)
            for n, h in enumerate(LEVELS):
                if n >= 2:
                    pool.wait_ge(gla_done, n)
                take_part(pool, gk_l[n % 2], gk[:, 1, :], gex[1], h, 1).then_inc(gla_ready[1], 1)
                pool.wait_ge(gla_ready[1], n + 1)
                if h < 128:
                    link(grow(pool, gex[1], 1, h, 1))
                    pool.wait_ge(gla_ready[0], n + 1)
                    grow(pool, fT[1], 1, h, 0).then_inc(ahead_grown, 1)
                    pool.wait_ge(ahead_grown, n + 1)
            pool.wait_ge(mod_gathered, 2)
            pool.memset(mod_acc[:], 0.0).then_inc(acc_zeroed, 1)
            head(1, ADA2)
            pool.wait_ge(mod_gathered, 3)
            pool.memset(mod_acc[:], 0.0).then_inc(acc_zeroed, 1)
            with pool.Fori(0, KT) as k:
                for q in (0, 1):
                    tile_in(1, k, 2048 + q * 1024, q, k, ADA3 // 2)
            with pool.Fori(0, KT // 2) as k:
                for q in (2, 3):
                    tile_in(1, k, 2048 + q * 1024, q % 2, k, ADA3 // 2 + KT)
            pool.wait_ge(z_evicted, N_EI + N_OI)
            pool.wait_ge(s_odd, 32)
            u = zo[:, 18:20, :].rearrange("p u (g t) -> p (u g) t", g=2)
            link(pool.memset(pu[:], 0.0))
            link(pool.tensor_copy(pu[:, :, 8:8 + T], u))
            s2, s4, s8 = pw
            link(pool.tensor_tensor(s2[:, :, 1:272], pu[:, :, 0:271], pu[:, :, 1:272], ALU.add))
            link(pool.tensor_tensor(s4[:, 1:4, 2:271], s2[:, 1:4, 1:270], s2[:, 1:4, 3:272], ALU.add))
            link(pool.tensor_tensor(s8[:, 2:4, 4:269], s4[:, 2:4, 2:267], s4[:, 2:4, 6:271], ALU.add))
            link(pool.tensor_tensor(s4[:, 3, 8:264], s8[:, 3, 4:260], s8[:, 3, 12:268], ALU.add))
            for g, s in enumerate((s2, s4, s8, s4)):
                link(pool.tensor_tensor(pmean[:, g, :], s[:, g, 8:8 + T], consts[:, C_INV + g * T:C_INV + (g + 1) * T],
                                        ALU.mult))
            pool.tensor_tensor(pmean[:], pmean[:], u, ALU.subtract).then_inc(pool_step, 1)

        POOL_STEPS = len(LEVELS) - 1 + 11

        @block.scalar
        def _(act):
            def split_hi(i, n, parts=(0, 1)):
                if isinstance(i, int) and n >= UNITS:
                    return
                if not isinstance(i, int) or n >= SPLIT:
                    act.wait_ge(w_used, i * 4 + n - SPLIT + 1)
                act.wait_ge(w_landed[n % RAW], (i + n // RAW + 1) * 32)
                for half in parts:
                    part = slice(half * UNIT // 2, (half + 1) * UNIT // 2)
                    nc.scalar.activation(w_hi[:, n % SPLIT, part], w_raw[:, n % RAW, part], ACT.Copy).then_inc(s_hi, 1)

            def squares(idx, first=0, last=KT):
                for k in range(first, last):
                    if idx == 0:
                        act.wait_ge(x_ready, k // 2 + 1)
                    else:
                        act.wait_ge(x_updated, KT * (idx - 1) + k + 1)
                    nc.scalar.activation(squared[idx][:, k, :], xT[:, k, :], ACT.Square).then_inc(norm_sq, 1)

            def rms(idx):
                act.wait_ge(norm_sum, idx + 1)
                nc.scalar.activation(rstd[:], aux[:, 0, 0:T], ACT.Sqrt, bias=consts[:, C_EPS:C_EPS + 1]).then_inc(
                    rms_ready, 1)

            def norm(idx, shift):
                for k in range(KT):
                    act.wait_ge(norm_mul, idx * KT + k + 1)
                    nc.scalar.activation(h_hi[:, k, :], work[:, k, :], ACT.Identity,
                                         bias=shift[:, k:k + 1]).then_inc(h_hi_ready, 1)

            def preload(func):
                nc.scalar.activation(table_sink[:], consts[:, C_EPS:C_EPS + 1], func)

            act.wait_ge(rows_turned, 1)
            nc.scalar.activation(vecs[:, 0:V_ALL], aux[:, 0, 0:V_ALL], ACT.Copy).then_inc(vecs_ready, 1)
            act.wait_ge(vecs_ready, 1)
            nc.scalar.activation(cact[:], vecs[:, V_C:V_C + KT], ACT.Silu).then_inc(cact_ready, 1)
            for b in range(4):
                act.wait_ge(x_turned, b + 1)
                nc.scalar.activation(xT[:, 2 * b:2 * b + 2, :].rearrange("p k t -> p (k t)"), big[:, b, :],
                                     ACT.Copy).then_inc(x_ready, 1)
            act.wait_ge(s_ident, 16)
            squares(0)
            rms(0)
            split_hi(0, 0)
            split_hi(0, 1)
            norm(0, mods[:, 0, 0:8])

            def in_step(first, zbuf, scale):
                def step(i, n):
                    act.wait_ge(w_used, i * 4 + n + 1)
                    to = zbuf[:, bass.ds(i * 4 + (n - first), 1), :].rearrange("p u n -> p (u n)")
                    nc.scalar.activation(to, acc[:, (n - first) % 2, :], ACT.Copy, scale=scale).then_inc(z_evicted, 1)
                    if isinstance(i, int) and n + SPLIT in (EO, EO + 1):
                        return
                    split_hi(i, n + SPLIT)
                return step

            stream(act, EI, 12, 4, in_step(EI, ze, 1.0))
            act.wait_ge(lb_diff, 1)
            nc.scalar.activation(lbt[:, 1, :], lbt[:, 0, :], ACT.Exp).then_inc(lb_exp, 1)
            act.wait_ge(z_evicted, 10)
            for n in range(EI + 12, EI + N_EI):
                in_step(EI, ze, 1.0)(0, n)
                d = n - EI - 12
                if d == 0:
                    act.wait_ge(bias_kept, 6)
                if d < 2:
                    nc.scalar.activation(gk[:, d, :], fT[d], ACT.Sigmoid, scale=-1.0).then_inc(gate_act, 1)
                    act.wait_ge(gate_act, 2 * d + 1)
                    nc.scalar.activation(fT[d], fT[d], ACT.Sigmoid).then_inc(gate_act, 1)
                elif d == 2:
                    nc.scalar.activation(qT, qT, ACT.Silu).then_inc(gate_act, 1)

            def attend(base, scores, kept, tokens, placed, beside=lambda s: None):
                width = scores.shape[2]
                for s in range(STEPS + 7):
                    if s < STEPS:
                        act.wait_ge(shifted, base + s + 1)
                        nc.scalar.activation(scores[:, s % 4, :], scores[:, s % 4, :], ACT.Exp,
                                             bias=stat[:, s % 4, 1:2], accum_out=stat[:, s % 4, 2:3]).then_inc(exp_done, 1)
                    if 0 <= s - 2 < STEPS:
                        r = s - 2
                        act.wait_ge(turned, base + r + 1)
                        if r >= 2:
                            act.wait_ge(attended, base + r - 1)
                        nc.scalar.activation(kept[:, r % 2, :], aux[:, r % 2, 0:width], ACT.Copy).then_inc(probs_kept, 1)
                    if s >= 7 and (s - 6) % 2:
                        j = (s - 6) // 2
                        act.wait_ge(out_turned, base // 2 + j + 1)
                        nc.scalar.activation(placed(j), tokens(big[:, 3, 0:P]), ACT.Copy).then_inc(out_placed, 1)
                    beside(s)

            attend(0, ns, npt, lambda a: a, lambda j: work[:, 4 + j // 2, (j % 2) * P:(j % 2 + 1) * P])
            nc.scalar.activation(gT, gT, ACT.Silu).then_inc(gate_act, 1)
            preload(ACT.Sqrt)
            act.wait_ge(gla_done, GLA_STEPS)
            flat = att[0:SB].rearrange("p h t n -> p h (t n)")
            for cols in (slice(SB, 6 * SB), slice(7 * SB, 8 * SB)):
                nc.scalar.activation(flat[:, :, cols], big[0:SB, :, cols], ACT.Copy).then_inc(att_copied, 1)
            act.wait_ge(out_placed, STEPS // 2)
            nc.scalar.activation(h_hi[:, 4:8, :], work[:, 4:8, :], ACT.Copy).then_inc(h_hi_ready, 1)
            split_hi(0, EO)
            for b in (0, 1):
                act.wait_ge(gla_out, b + 1)
                nc.scalar.activation(work[:, 2 * b:2 * b + 2, :].rearrange("p k t -> p (k t)"), acc[:, b, :],
                                     ACT.Copy).then_inc(gla_sq, 1)
                nc.scalar.activation(gq_l[1][:, b * 512:(b + 1) * 512], acc[:, b, :], ACT.Square).then_inc(gla_sq, 1)
            for b in (0, 1):
                act.wait_ge(gla_mean, b + 1)
                nc.scalar.activation(gk_l[1][:, b * 512:(b + 1) * 512], aux[:, b, :], ACT.Sqrt,
                                     bias=consts[:, C_EPS:C_EPS + 1]).then_inc(gla_rms, 1)
            split_hi(0, EO + 1)
            act.wait_ge(gla_normed, 2)
            nc.scalar.activation(h_hi[:, 0:4, :], work[:, 0:4, :], ACT.Copy).then_inc(h_hi_ready, 1)

            def out_projection(first, idx):
                for n in range(first, first + N_EO):
                    if n < first + N_EO - 1:
                        split_hi(0, n + SPLIT)
                    squares(idx, 2 * (n - first), 2 * (n - first) + 2)
                rms(idx)
                split_hi(0, first + N_EO - 1 + SPLIT)

            def ffn(l, first_up, first_down, idx):
                norm(idx, mods[:, l, 24:32])

                def up_step(i, n):
                    u = n - first_up
                    a = u % 2
                    nu = i * 4 + (l * FT + u)
                    if u % 4 == 0:
                        preload(ACT.Silu)
                    act.wait_ge(w_used, i * 4 + n + 1)
                    nc.scalar.activation(conv[:, a, :], acc[:, a, 0:T], ACT.Identity,
                                         bias=vecs[:, bass.ds(i * 4 + (V_CB + l * FT + u), 1)],
                                         scale=vecs[:, bass.ds(i * 4 + (V_CW + l * 3 * FT + FT + u), 1)]
                                         ).then_inc(conv_mid, 1)
                    split_hi(i, n + SPLIT, (0,))
                    act.wait_ge(conv_taps, nu * 2 + 2)
                    nc.scalar.activation(gated[:, a, :], conv[:, a, :], ACT.Silu).then_inc(silu_ready, 1)
                    split_hi(i, n + SPLIT, (1,))
                    act.wait_ge(hid_ready, nu + 1)
                    nc.scalar.activation(hid_hi[:, bass.ds(i * 4 + u, 1), :].rearrange("p u n -> p (u n)"),
                                         hid[:, a, :], ACT.Copy).then_inc(hid_hi_ready, 1)
                stream(act, first_up, N_UP, 4, up_step)
                preload(ACT.Sqrt)
                stream(act, first_down, N_DN, 4, lambda i, n: split_hi(i, n + SPLIT)) if l == 0 else \
                    stream(act, first_down, N_DN - SPLIT, 4, lambda i, n: split_hi(i, n + SPLIT))

            out_projection(EO, 1)
            ffn(0, UP0, DN0, 1)

            squares(2)
            rms(2)
            norm(2, mods[:, 1, 0:8])
            stream(act, OI, 6, 4, in_step(OI, zo, SCALE))
            act.wait_ge(h_lo_ready, NORM_AT[2] + KT)
            for to, frm in ((wrap_hi, h_hi), (wrap_lo, h_lo)):
                nc.scalar.activation(to[:, :, 0:64], frm[:, :, 3 * 64:4 * 64].bitcast(F32), ACT.Copy).then_inc(wrapped, 1)
                nc.scalar.activation(to[:, :, 64:128], frm[:, :, 0:64].bitcast(F32), ACT.Copy).then_inc(wrapped, 1)
            stream(act, OI + 6, 8, 4, in_step(OI, zo, 1.0))
            for n in range(OI + 14, OI + 18):
                u = n - OI
                a = u % 2
                act.wait_ge(w_used, n + 1)
                for side in (0, 1):
                    lane = slice(64 * side, 64 * side + 64)
                    for t in range(TT):
                        residue = (2 * t + side + (0 if u < 16 else 1)) % RES
                        ins = nc.scalar.activation(zo[lane, 14 + residue, a * 256:(a + 1) * 256],
                                                   acc[lane, a, t * T:(t + 1) * T], ACT.Copy)
                ins.then_inc(z_evicted, 1)
                split_hi(0, n + SPLIT)
            for n in range(OI + 18, OI + N_OI):
                act.wait_ge(w_used, n + 1)
                nc.scalar.activation(zo[:, n - OI, :].rearrange("p (g b r) -> p g r b", g=2, r=RES),
                                     acc[:, n % 2 ^ OI % 2, :].rearrange("p (g r b) -> p g r b", g=2, r=RES),
                                     ACT.Copy).then_inc(z_evicted, 1)

            by_residue = lambda a: a.rearrange("p (b r) -> p r b", r=RES)
            attend(STEPS, cs, cpt, lambda a: a.rearrange("p (r b) -> p r b", r=2),
                   lambda j: by_residue(work[:, j // 2, :])[:, 2 * (j % 2):2 * (j % 2) + 2, :],
                   lambda s: split_hi(0, OO + s // 4 - 1) if s in (4, 8) else None)
            preload(ACT.Sqrt)
            act.wait_ge(out_placed, STEPS)
            nc.scalar.activation(h_hi[:, 0:4, :], work[:, 0:4, :], ACT.Copy).then_inc(h_hi_ready, 1)
            act.wait_ge(pool_mixed, 1)
            for g in range(4):
                nc.scalar.activation(work[:, 4 + g, :], big[:, g // 2, (g % 2) * T:(g % 2 + 1) * T], ACT.Copy,
                                     scale=vecs[:, V_PSC + g:V_PSC + g + 1]).then_inc(pool_taken, 1)
            act.wait_ge(pool_taken, 4)
            nc.scalar.activation(h_hi[:, 4:8, :], work[:, 4:8, :], ACT.Copy).then_inc(h_hi_ready, 1)
            out_projection(OO, 3)
            ffn(1, UP1, DN1, 3)

            squares(4)
            rms(4)
            for half, t in ((0, 0), (0, 1), (1, 0)):
                act.wait_ge(y_turned, half + 1)
                nc.scalar.activation(y_tok[:, t, half * 512:(half + 1) * 512], big[:, 2 * t + half, :],
                                     ACT.Copy).then_inc(y_copied[t], 1)

        @block.vector
        def _(dve):
            chained = [0]

            def link(ins):
                chained[0] += 1
                ins.then_inc(dve_chain, 1)
                dve.wait_ge(dve_chain, chained[0])

            def split_lo(i, n, parts=(0, 1)):
                if isinstance(i, int) and n >= UNITS:
                    return
                for half in parts:
                    part = slice(half * UNIT // 2, (half + 1) * UNIT // 2)
                    dve.wait_ge(s_hi, i * 8 + 2 * n + half + 1)
                    dve.tensor_tensor(w_lo[:, n % SPLIT, part], w_raw[:, n % RAW, part],
                                      w_hi[:, n % SPLIT, part].bitcast(F32), ALU.subtract).then_inc(s_lo, 1)

            def add_tile(k, q, slot, i2, t2, landed=ada_landed, before=ADA1):
                dve.wait_ge(ada_used, i2 * 2 + 2 * t2 + slot - 1)
                if before == ADA1 and t2 >= ADA2 // 2:
                    before += 12
                dve.wait_ge(landed[slot], (i2 + t2 + 1 - before // 2) * 16)
                sums = mod_acc[:, q * 1024:(q + 1) * 1024]
                dve.scalar_tensor_tensor(out=sums, in0=ada_raw[:, slot, :], scalar=cact[:, bass.ds(k, 1)], in1=sums,
                                         op0=ALU.mult, op1=ALU.add).then_inc(ada_used, 1)

            def keep_mods(e, count, bank):
                dve.wait_ge(mod_gathered, e + 1)
                dve.tensor_copy(mod_rows[0:count, :], bank[0:count, 0:P]).then_inc(mod_kept, 1)

            def take_mods(e, l, first, count, bank):
                dve.wait_ge(mod_summed, e + 1)
                cols = slice(V_ADAB + 48 * l + first, V_ADAB + 48 * l + first + count)
                dve.tensor_tensor(mods[:, l, first:first + count], bank[:, P:P + count], vecs[:, cols],
                                  ALU.add).then_inc(mod_ready, 1)
                dve.wait_ge(mod_ready, e + 1)

            def make_gain(idx, l, first, v):
                dve.scalar_tensor_tensor(out=gain[:, idx, :], in0=mods[:, l, first:first + KT], scalar=1.0,
                                         in1=vecs[:, v:v + KT], op0=ALU.add, op1=ALU.mult).then_inc(gain_ready, 1)

            def reciprocal_rms(idx):
                dve.wait_ge(rms_ready, idx + 1)
                dve.reciprocal(rstd[:], rstd[:]).then_inc(rstd_ready, 1)
                dve.wait_ge(rstd_ready, idx + 1)

            LAG = 2

            def norm(idx, shift, order=lambda a: (a, a)):
                if idx:
                    reciprocal_rms(idx)
                dve.wait_ge(gain_ready, idx + 1)
                for step in range(KT + LAG):
                    if step < KT:
                        dve.scalar_tensor_tensor(out=order(work[:, step, :])[0], in0=order(xT[:, step, :])[1],
                                                 scalar=gain[:, idx, step:step + 1], in1=order(rstd[:])[1], op0=ALU.mult,
                                                 op1=ALU.mult).then_inc(norm_mul, 1)
                    if step < LAG:
                        continue
                    k = step - LAG
                    dve.wait_ge(h_hi_ready, NORM_AT[idx] + k + 1)
                    dve.scalar_tensor_tensor(out=h_lo[:, k, :], in0=work[:, k, :], scalar=shift[:, k:k + 1],
                                             in1=h_hi[:, k, :].bitcast(F32), op0=ALU.add,
                                             op1=ALU.subtract).then_inc(h_lo_ready, 1)

            def mixed_lo(value, half):
                part = slice(4 * half, 4 * half + 4)
                dve.wait_ge(h_hi_ready, value)
                dve.tensor_tensor(h_lo[:, part, :], work[:, part, :], h_hi[:, part, :].bitcast(F32),
                                  ALU.subtract).then_inc(h_lo_ready, 1)

            dve.wait_ge(cact_ready, 1)
            sums = mod_acc[:, 0:2048]
            for k in range(KT):
                dve.wait_ge(first_landed[k], 16)
                if k == 0:
                    dve.tensor_scalar(sums, ada_first[k], cact[:, 0:1], None, ALU.mult).then_inc(ada_used, 1)
                else:
                    dve.wait_ge(ada_used, k)
                    dve.scalar_tensor_tensor(out=sums, in0=ada_first[k], scalar=cact[:, k:k + 1], in1=sums,
                                             op0=ALU.mult, op1=ALU.add).then_inc(ada_used, 1)
            reciprocal_rms(0)
            split_lo(0, 0)
            keep_mods(0, 16, aux[:, 1])
            take_mods(0, 0, 0, 16, aux[:, 1])
            make_gain(0, 0, 8, V_NMIX)
            norm(0, mods[:, 0, 0:8])
            split_lo(0, 1)
            logits = vecs[:, V_LB:V_LB + A_HEADS]
            dve.tensor_tensor(lbt[:, 0, :], logits, logits, ALU.subtract).then_inc(lb_diff, 1)

            dve.wait_ge(acc_zeroed, 1)

            def in_step(first, base, tile0, per):
                def step(i, n):
                    if not (isinstance(i, int) and n + SPLIT in (EO, EO + 1, OO, OO + 1)):
                        split_lo(i, n + SPLIT)
                    for tile in range(tile0 + per * (n - first), tile0 + per * (n - first + 1)):
                        add_tile(i * per + tile // 4, tile % 4, tile % 2, i * 2 * per, base // 2 + tile // 2)
                return step
            def keep_bias(first, last):
                for b in range(first, last):
                    dve.wait_ge(bias_turned, b + 1)
                    mask = consts[:, C_NAT:C_NAT + GRID_W].unsqueeze(1).to_broadcast([P, 8, GRID_W])
                    dve.tensor_tensor(nbias[:].rearrange("p h e c -> p (h e) c")[:, 8 * b:8 * b + 8, :],
                                      big[:, b % 4, :].rearrange("p (e c) -> p e c", c=GRID_W), mask,
                                      ALU.add).then_inc(bias_kept, 1)

            stream(dve, EI, 8, 4, in_step(EI, ADA1, 0, 1))
            stream(dve, EI + 8, 2, 4, in_step(EI + 8, ADA1, 8, 2))
            dve.wait_ge(s_const, 16)
            keep_bias(0, 4)
            stream(dve, EI + 10, 2, 4, in_step(EI + 8, ADA1, 8, 2))
            keep_bias(4, 6)
            for n, tile, count in ((12, 16, 2), (13, 18, 1), (14, 19, 1), (15, 20, 0)):
                in_step(EI + n, ADA1, tile, count)(0, EI + n)
            dve.wait_ge(lb_exp, 1)
            link(dve.reciprocal(lbt[:, 2, :], lbt[:, 1, :]))
            link(dve.tensor_tensor(lbt[:, 3, :], lbt[:, 1, :], lbt[:, 2, :], ALU.mult))
            link(dve.tensor_tensor(lbt[:, 0, :], lbt[:, 3, :], lbt[:, 3, :], ALU.subtract))
            dve.tensor_scalar(lbt[:, 4, :], lbt[:, 0, :], LB_FLOOR, None, ALU.max)
            dve.tensor_scalar(lbt[:, 5, :], lbt[:, 0, :], -1.0, 1.0, ALU.mult, ALU.add).then_inc(lb_ready, 1)

            def attend(base, scores, tok, shift, beside=lambda s: None):
                for s in range(STEPS + 4):
                    if s >= 4:
                        r = s - 4
                        j = r // 2
                        dve.wait_ge(exp_done, base + r + 1)
                        link(dve.reciprocal(stat[:, r % 4, 3:4], stat[:, r % 4, 2:3]))
                        dve.wait_ge(attended, base + r + 1)
                        if r % 2 == 0 and j >= 2:
                            dve.wait_ge(out_turned, base // 2 + j - 1)
                        dve.tensor_scalar(tok[:, j % 2, (r % 2) * DH:(r % 2 + 1) * DH], acc[:, r % 2, 0:DH],
                                          stat[:, r % 4, 3:4], None, ALU.mult).then_inc(out_taken, 1)
                    if s < STEPS:
                        dve.wait_ge(scored, base + s + 1)
                        if s >= 4:
                            dve.wait_ge(turned, base + s - 3)
                        link(shift(s, 2 * (s // 4) + s % 2, s // 2 % 2))
                        link(dve.tensor_reduce(stat[:, s % 4, 0:1], scores[:, s % 4, :], AX_X, ALU.max))
                        dve.tensor_scalar(stat[:, s % 4, 1:2], stat[:, s % 4, 0:1], -1.0, None,
                                          ALU.mult).then_inc(shifted, 1)
                    beside(s)

            def nat_shift(s, h, t):
                e = 2 - 2 * t
                return dve.scalar_tensor_tensor(out=ns[:, s % 4, :], in0=big[:, s % 3, 0:T], scalar=SCALE,
                                                op0=ALU.mult, op1=ALU.add,
                                                in1=nbias[:, h, e:e + 4, :].rearrange("p e c -> p (e c)"))

            def dil_shift(s, h, t):
                for at0, at1, k in ((0, T, -slope(0, h)),
                                    (T, T + 64, consts[:, C_SLOPE + 2 * h:C_SLOPE + 2 * h + 1]),
                                    (T + 64, ROW, consts[:, C_SLOPE + 2 * h + 1:C_SLOPE + 2 * h + 2])):
                    col = C_DIST + t * ROW
                    ins = dve.scalar_tensor_tensor(out=cs[:, s % 4, at0:at1], in0=consts[:, col + at0:col + at1],
                                                   scalar=k, in1=big[:, s % 3, at0:at1], op0=ALU.mult, op1=ALU.add)
                return ins

            def add_rest(tile):
                add_tile(tile // 4, tile % 4, tile % 2, 0, (ADA1 + tile) // 2, rest_landed, ADA1 + 20)

            def later_tiles(s):
                if s < STEPS + 2 and s % 2:
                    add_rest(20 + s // 2)

            attend(0, ns, ntok, nat_shift, later_tiles)
            def take_diag(s):
                dve.wait_ge(gla_done, s + 1)
                src = diag_banks[s % 4].rearrange("p (b q) -> p b q", q=SB)
                if s == 0:
                    dve.tensor_copy(diag[:], src).then_inc(diag_taken, 1)
                else:
                    dve.wait_ge(diag_taken, s)
                    col = C_LVL + (s - 1) * SB
                    mask = consts[:, col:col + SB].bitcast(I32).unsqueeze(1).to_broadcast([P, A_HEADS * TT, SB])
                    dve.copy_predicated(diag[:], mask, src).then_inc(diag_taken, 1)

            dve.wait_ge(gates_ready, 1)
            dve.wait_ge(gate_act, 5)
            dve.wait_ge(gla_cleared, 2)
            for n, h in enumerate(LEVELS):
                if n >= 2:
                    dve.wait_ge(gla_done, n)
                take_part(dve, gq_l[n % 2], qT, fT[0], h, 1)
                take_part(dve, gk_l[n % 2], gk[:, 0, :], gex[0], h, 0)
                if n >= 1:
                    dve.wait_ge(ahead_grown, n)
                take_part(dve, gq_l[n % 2], qT, fT[1], h, 0).then_inc(gla_ready[0], 1)
                dve.wait_ge(gla_ready[0], n + 1)
                if h < 128:
                    link(grow(dve, gex[0], 0, h, 0))
                    link(grow(dve, fT[0], 0, h, 1))
                if n == 7:
                    add_rest(29)
                if n < SMALL:
                    take_diag(n)
            dve.wait_ge(gla_done, GLA_STEPS)
            flat = att[SB:P].rearrange("p h t n -> p h (t n)")
            for cols in (slice(0, SB), slice(2 * SB, 7 * SB)):
                dve.tensor_copy(flat[:, :, cols], big[SB:P, :, cols])
            dve.wait_ge(diag_taken, SMALL)
            for q in range(P // SB):
                rows = slice(SB * q, SB * (q + 1))
                for t in range(TT):
                    ins = dve.tensor_copy(att[rows, :, t, t * P + SB * q:t * P + SB * (q + 1)],
                                          diag[rows].rearrange("p (h t) q -> p h t q", t=TT)[:, :, t, :])
            ins.then_inc(att_ready, 1)
            mixed_lo(MIX_AT[0] + 1, 1)
            add_rest(30)
            add_rest(31)
            split_lo(0, EO)
            for b in (0, 1):
                part = slice(b * 512, (b + 1) * 512)
                o = work[:, 2 * b:2 * b + 2, :].rearrange("p k t -> p (k t)")
                dve.wait_ge(gla_rms, b + 1)
                link(dve.reciprocal(gk_l[1][:, part], gk_l[1][:, part]))
                link(dve.scalar_tensor_tensor(out=o, in0=o, scalar=vecs[:, V_HG:V_HG + 1], in1=gk_l[1][:, part],
                                              op0=ALU.mult, op1=ALU.mult))
                dve.wait_ge(gate_act, 6)
                dve.tensor_tensor(o, o, gT[:, part], ALU.mult).then_inc(gla_normed, 1)
            keep_mods(1, 32, big[:, 0])
            mixed_lo(MIX_AT[0] + 2, 0)
            split_lo(0, EO + 1)
            take_mods(1, 0, 16, 32, big[:, 0])
            make_gain(1, 0, 32, V_NFFN)

            def out_projection(l, first):
                for n in range(first, first + N_EO):
                    dve.wait_ge(w_used, n + 1)
                    for g in (0, 1):
                        k = 2 * (n - first) + g
                        dve.scalar_tensor_tensor(out=xT[:, k, :], in0=acc[:, (n - first) % 2, g * T:(g + 1) * T],
                                                 scalar=mods[:, l, 16 + k:17 + k], in1=xT[:, k, :], op0=ALU.mult,
                                                 op1=ALU.add).then_inc(x_updated, 1)
                    if n < first + N_EO - 1:
                        split_lo(0, n + SPLIT)

            def ffn(l, first_up, first_down, idx):
                norm(idx, mods[:, l, 24:32])
                split_lo(0, first_up + 1)
                if l == 0:
                    dve.wait_ge(acc_zeroed, 2)

                def up_step(adding):
                    def step(i, n):
                        u = n - first_up
                        a = u % 2
                        nu = i * 4 + (l * FT + u)
                        tap = lambda j: vecs[:, bass.ds(i * 4 + (V_CW + l * 3 * FT + j * FT + u), 1)]
                        dve.wait_ge(conv_mid, nu + 1)
                        dve.scalar_tensor_tensor(out=conv[:, a, 1:T], in0=acc[:, a, 0:T - 1], scalar=tap(0),
                                                 in1=conv[:, a, 1:T], op0=ALU.mult, op1=ALU.add).then_inc(conv_taps, 1)
                        dve.wait_ge(conv_taps, nu * 2 + 1)
                        dve.scalar_tensor_tensor(out=conv[:, a, 0:T - 1], in0=acc[:, a, 1:T], scalar=tap(2),
                                                 in1=conv[:, a, 0:T - 1], op0=ALU.mult, op1=ALU.add).then_inc(conv_taps, 1)
                        split_lo(i, n + SPLIT, (0,))
                        dve.wait_ge(silu_ready, nu + 1)
                        dve.tensor_tensor(hid[:, a, :], gated[:, a, :], acc[:, a, T:2 * T], ALU.mult).then_inc(hid_ready, 1)
                        split_lo(i, n + SPLIT, (1,))
                        if adding:
                            add_tile(i * 2 + u // 2, u % 2, u % 2, i * 2, ADA2 // 2 + u // 2)
                        dve.wait_ge(hid_hi_ready, nu + 1)
                        dve.tensor_tensor(hid_lo[:, bass.ds(i * 4 + u, 1), :].rearrange("p u n -> p (u n)"),
                                          hid[:, a, :],
                                          hid_hi[:, bass.ds(i * 4 + u, 1), :].rearrange("p u n -> p (u n)").bitcast(F32),
                                          ALU.subtract).then_inc(hid_lo_ready, 1)
                    return step
                if l == 0:
                    stream(dve, first_up, 16, 4, up_step(True))
                    for n in range(first_up + 16, first_up + N_UP):
                        up_step(False)(0, n)
                else:
                    stream(dve, first_up, N_UP, 4, up_step(False))
                stream(dve, first_down, N_DN if l == 0 else N_DN - SPLIT, 4, lambda i, n: split_lo(i, n + SPLIT))
                for k in range(KT):
                    if k < KT - 2:
                        dve.wait_ge(down_summed, 3 * l + k // 2 + 1)
                    else:
                        dve.wait_ge(w_used, first_down + N_DN)
                    dve.scalar_tensor_tensor(out=xT[:, k, :], in0=big[:, k // 2, (k % 2) * T:(k % 2 + 1) * T],
                                             scalar=mods[:, l, 40 + k:41 + k], in1=xT[:, k, :], op0=ALU.mult,
                                             op1=ALU.add).then_inc(x_updated, 1)

            out_projection(0, EO)
            ffn(0, UP0, DN0, 1)
            keep_mods(2, 16, aux[:, 1])
            take_mods(2, 1, 0, 16, aux[:, 1])
            make_gain(2, 1, 8, V_NMIX + KT)
            norm(2, mods[:, 1, 0:8], order=lambda a: (a.rearrange("p (r b) -> p b r", r=RES),
                                                      a.rearrange("p (b r) -> p b r", r=RES)))
            dve.wait_ge(acc_zeroed, 3)
            def late_step(first, tile0, per):
                def step(i, n):
                    if not (isinstance(i, int) and n + SPLIT in (OO, OO + 1)):
                        split_lo(i, n + SPLIT)
                    for tile in range(tile0 + per * (n - first), tile0 + per * (n - first + 1)):
                        add_tile(i * 2 * per + tile % 16 // 2, 2 * (tile // 16) + tile % 2, tile % 2, i * 2 * per,
                                 (ADA3 + tile) // 2)
                return step

            stream(dve, OI, 4, 4, late_step(OI, 0, 2))
            stream(dve, OI + 4, 8, 4, late_step(OI + 4, 8, 1))
            stream(dve, OI + 12, 4, 4, late_step(OI + 12, 16, 1))
            stream(dve, OI + 16, 4, 4, late_step(OI + 12, 16, 1))
            dve.wait_ge(s_odd, 32)

            def beside_dilated(s):
                if s == 2:
                    keep_mods(3, 32, acc[:, 1])
                if s in (8, 12):
                    split_lo(0, OO + s // 4 - 2)
                if s >= 3 and s % 2:
                    tile = 24 + (s - 3) // 2
                    if tile < 32:
                        add_tile(tile % 16 // 2, 2 + tile % 2, tile % 2, 0, (ADA3 + tile) // 2, rest_landed,
                                 ADA3 + 24 - 12)

            attend(STEPS, cs, ctok, dil_shift, beside_dilated)
            mixed_lo(MIX_AT[1] + 1, 0)
            dve.wait_ge(mod_kept, 4)
            dve.wait_ge(mod_gathered, 5)
            dve.tensor_tensor(mod_rows[:], mod_rows[:], acc[0:32, 1, 0:P], ALU.add).then_inc(mod_kept, 1)
            mixed_lo(MIX_AT[1] + 2, 1)
            take_mods(3, 1, 16, 32, big[:, 3])
            make_gain(3, 1, 32, V_NFFN + KT)
            out_projection(1, OO)
            ffn(1, UP1, DN1, 3)

            reciprocal_rms(4)
            for k in range(KT):
                dve.scalar_tensor_tensor(out=work[:, k, :], in0=xT[:, k, :], scalar=vecs[:, V_FIN + k:V_FIN + k + 1],
                                         in1=rstd[:], op0=ALU.mult, op1=ALU.mult).then_inc(y_ready, 1)
            dve.wait_ge(y_turned, 2)
            dve.tensor_copy(y_tok[:, 1, 512:], big[:, 3, :]).then_inc(y_copied[1], 1)

        @block.tensor
        def _(pe):
            def three(dst, w, h, start, stop, swap=False):
                for n, (a, b) in enumerate(((w[0], h[0]), (w[0], h[1]), (w[1], h[0]))):
                    lhsT, rhs = (b, a) if swap else (a, b)
                    ins = pe.matmul(dst, lhsT, rhs, start=start and n == 0, stop=stop and n == 2, skip_group_check=True)
                return ins

            def split_ready(i, per, n):
                pe.wait_ge(s_lo, i * (2 * per) + 2 * n + 2)

            def feature_major(n, a, h_from=None, order=range(KT), per=1):
                steps = [(k, g) for k in order for g in (0, 1)] if h_from is not None else \
                    [(k, g) for g in (0, 1) for k in range(KT)]
                for count, (k, g) in enumerate(steps):
                    if h_from is not None and count % (2 * per) == 0:
                        pe.wait_ge(h_lo_ready, h_from + count // (2 * per) + 1)
                    cols = slice(k * 256 + g * P, k * 256 + (g + 1) * P)
                    ins = three(acc[:, a, g * T:(g + 1) * T], (w_hi[:, n % SPLIT, cols], w_lo[:, n % SPLIT, cols]),
                                (h_hi[:, k, :], h_lo[:, k, :]), count == 0 if h_from is not None else k == 0,
                                count >= len(steps) - 2 if h_from is not None else k == KT - 1)
                ins.then_inc(w_used, 1)

            def token_major(n, a, order=None):
                for t in range(TT):
                    for k in range(KT):
                        cols = slice(k * 256, (k + 1) * 256)
                        hk = order(k, t) if order else (h_hi[:, k, t * P:(t + 1) * P], h_lo[:, k, t * P:(t + 1) * P])
                        ins = three(acc[:, a, t * T:(t + 1) * T], (w_hi[:, n % SPLIT, cols], w_lo[:, n % SPLIT, cols]),
                                    hk, k == 0, k == KT - 1, swap=True)
                ins.then_inc(w_used, 1)

            def staggered(k, t):
                return (h_hi[:, k, 64:192], h_lo[:, k, 64:192]) if t == 0 else (wrap_hi[:, k, :], wrap_lo[:, k, :])

            def units(first, start, count, form, freed, freed_base, fresh=2, h_from=None):
                def step(i, n):
                    split_ready(i, 2, n)
                    if not isinstance(i, int) or n - first >= fresh:
                        pe.wait_ge(freed, i * (2 * freed_per) + (freed_base + (n - first) * freed_per - freed_per))
                    form(n, (n - first) % 2, **({"h_from": h_from} if h_from is not None and n == start else {}))
                freed_per = 2 if freed is x_updated else 1
                head = min(count, max(0, first + fresh - start))
                for n in range(start, start + head):
                    step(0, n)
                stream(pe, start + head, count - head, 2, step)

            def norm_sum_of(idx, first=0, last=KT):
                for k in range(first, last):
                    pe.wait_ge(norm_sq, KT * idx + k + 1)
                    ins = pe.matmul(aux[:, 0, 0:T], mean_w, squared[idx][:, k, :], start=(k == 0), stop=(k == KT - 1),
                                    skip_group_check=True)
                if last == KT:
                    ins.then_inc(norm_sum, 1)

            def mod_sum(e, tiles, count, bank, first=0, last=None):
                pe.wait_ge(ada_used, tiles)
                last = count if last is None else last
                for g in range(first, last):
                    pick = consts[:, C_PICK + 31 - g:C_PICK + 31 - g + count]
                    ins = pe.matmul(bank[0:count, 0:P], pick, mod_acc[:, g * P:(g + 1) * P], start=g == first,
                                    stop=g == last - 1)
                ins.then_inc(mod_gathered, 1)

            def mod_turn(e, count, bank):
                pe.wait_ge(mod_kept, e + 1 + (e == 3))
                pe.transpose(bank[:, P:P + count], mod_rows[0:count, :], ident[0:count, 0:count]).then_inc(mod_summed, 1)

            pe.wait_ge(s_ident, 16)
            pe.wait_ge(s_rows, 16 * 11)
            pe.transpose(aux[:, 0, 0:104], rows_a[:], ident[0:104, 0:104])
            pe.transpose(aux[:, 0, 104:197], rows_b[:], ident[0:93, 0:93])
            for l in (0, 1):
                at0 = V_CW + l * 3 * FT
                ins = pe.transpose(aux[:, 0, at0:at0 + 3 * FT], rows_c[:, l, :], ident[0:3 * FT, 0:3 * FT])
            ins.then_inc(rows_turned, 1)
            pe.wait_ge(s_x, 16)
            for b in range(4):
                for k in (2 * b, 2 * b + 1):
                    for t in range(TT):
                        to = (k % 2) * T + t * P
                        ins = pe.transpose(big[:, b, to:to + P], x_tok[:, t, k * P:(k + 1) * P], ident)
                ins.then_inc(x_turned, 1)
            norm_sum_of(0)
            mod_sum(0, ADA1, 16, aux[:, 1])
            mod_turn(0, 16, aux[:, 1])

            units(EI, EI, 6, feature_major, z_evicted, 0, h_from=NORM_AT[0])
            units(EI, EI + 6, 2, token_major, z_evicted, 0)

            def turn_bias(first, last):
                for b in range(first, last):
                    if b >= 4:
                        pe.wait_ge(bias_kept, b - 3)
                    pe.matmul(big[:, b % 4, :], consts[:, C_FLIP:C_FLIP + P],
                              nflip[:].rearrange("p h e c -> p (h e c)")[:, b * 512:(b + 1) * 512], start=True,
                              stop=True).then_inc(bias_turned, 1)

            units(EI, EI + 8, 2, feature_major, z_evicted, 0)
            pe.wait_ge(s_const, 16)
            pe.wait_ge(s_bias, 16 * 2 * NA_HEADS)
            turn_bias(0, 4)
            units(EI, EI + 10, 2, feature_major, z_evicted, 0)
            turn_bias(4, 6)
            units(EI, EI + 12, 2, feature_major, z_evicted, 0)
            units(EI, EI + 14, 2, token_major, z_evicted, 0)

            def attend(base, width, scores_of, values_of, kept, tok, values_at, beside=lambda s: None):
                for s in range(STEPS + 6):
                    if s < STEPS:
                        if s >= 3:
                            pe.wait_ge(shifted, base + s - 2)
                        scores_of(big[:, s % 3, :], 2 * (s // 4) + s % 2, s // 2 % 2).then_inc(scored, 1)
                    beside(s)
                    if 0 <= s - 2 < STEPS:
                        r = s - 2
                        pe.wait_ge(exp_done, base + r + 1)
                        if r >= 2:
                            pe.wait_ge(probs_kept, base + r - 1)
                        for j in range(width // P):
                            ins = pe.transpose(aux[:, r % 2, j * P:(j + 1) * P],
                                               (ns if base == 0 else cs)[:, r % 4, j * P:(j + 1) * P], ident)
                        ins.then_inc(turned, 1)
                    if 0 <= s - 3 < STEPS:
                        r = s - 3
                        if r == 0:
                            pe.wait_ge(z_evicted, values_at)
                        pe.wait_ge(probs_kept, base + r + 1)
                        if r >= 2:
                            pe.wait_ge(out_taken, base + r - 1)
                        values_of(acc[:, r % 2, 0:DH], kept[:, r % 2, :], 2 * (r // 4) + r % 2,
                                  r // 2 % 2).then_inc(attended, 1)
                    if s >= 6 and s % 2 == 0:
                        j = (s - 6) // 2
                        pe.wait_ge(out_taken, base + 2 * j + 2)
                        if j >= 1:
                            pe.wait_ge(out_placed, base // 2 + j)
                        pe.transpose(big[:, 3, 0:P], tok[:, j % 2, :], ident).then_inc(out_turned, 1)

            def nat_scores(bank, h, t):
                lane = slice((h % 2) * DH, (h % 2 + 1) * DH)
                cols = (h // 2 % 2) * T
                q = ze[lane, 10 + h // 4, cols + t * P:cols + (t + 1) * P]
                return pe.matmul(bank[:, 0:T], q, ze[lane, 12 + h // 4, cols:cols + T], start=True, stop=True)

            def nat_values(dst, probs, h, t):
                for kt in range(TT):
                    v = ze[:, 14 + h // 4, kt * T + (h % 4) * DH:kt * T + (h % 4 + 1) * DH]
                    ins = pe.matmul(dst, probs[:, kt * P:(kt + 1) * P], v, start=(kt == 0), stop=(kt == TT - 1))
                return ins

            pe.wait_ge(z_evicted, 14)
            attend(0, T, nat_scores, nat_values, npt, ntok, N_EI)

            for s in range(GLA_STEPS):
                if s == 0:
                    pe.wait_ge(own_ready, 1)
                    pe.wait_ge(gate_act, 5)
                    queries, keys = qT, gk_own
                else:
                    for ready in gla_ready:
                        pe.wait_ge(ready, s)
                    h = LEVELS[s - 1]
                    queries, keys = gq_l[(s - 1) % 2], gk_l[(s - 1) % 2]
                if s < SMALL:
                    if s >= 4:
                        pe.wait_ge(diag_taken, s - 3)
                    for hd in range(A_HEADS):
                        for b in range(T // SB):
                            toks = slice(hd * T + b * SB, hd * T + (b + 1) * SB)
                            row, col = (b % 2) * SB, (hd * TT + b // 2) * SB
                            ins = pe.matmul(diag_banks[s % 4][row:row + SB, col:col + SB], keys[:, toks], queries[:, toks],
                                            start=True, stop=True, skip_group_check=True)
                else:
                    pe.wait_ge(out_placed, STEPS // 2)
                    for hd in range(A_HEADS):
                        for b in range(T // (2 * h)):
                            for d in (0, 1):
                                left, right = 2 * h * b, 2 * h * b + h
                                ktok, qtok = (left, right) if d == 0 else (right, left)
                                row, t = ktok % P, ktok // P
                                ins = pe.matmul(big[row:row + h, hd, t * T + qtok:t * T + qtok + h],
                                                keys[:, hd * T + ktok:hd * T + ktok + h],
                                                queries[:, hd * T + qtok:hd * T + qtok + h], start=True, stop=True,
                                                skip_group_check=True)
                ins.then_inc(gla_done, 1)
            pe.wait_ge(att_copied, 2)
            pe.wait_ge(att_ready, 1)
            for b in (0, 1):
                for hd in (2 * b, 2 * b + 1):
                    for t in range(TT):
                        v = ze[:, 6 + hd // 2, t * T + (hd % 2) * P:t * T + (hd % 2 + 1) * P]
                        ins = pe.matmul(acc[:, b, (hd % 2) * T:(hd % 2 + 1) * T], v, att[:, hd, t, :], start=(t == 0),
                                        stop=(t == TT - 1))
                ins.then_inc(gla_out, 1)
            for b in (0, 1):
                pe.wait_ge(gla_sq, 2 * b + 2)
                pe.matmul(aux[:, b, :], hmean_w, gq_l[1][:, b * 512:(b + 1) * 512], start=True, stop=True).then_inc(
                    gla_mean, 1)
            mod_sum(1, ADA2, 32, big[:, 0])
            mod_turn(1, 32, big[:, 0])

            def ffn(l, first_up, first_down, idx):
                norm_sum_of(idx, 6)
                units(first_up, first_up, N_UP, feature_major, hid_ready, l * FT, h_from=NORM_AT[idx])
                def down_unit(i, n):
                    split_ready(i, 2, n)
                    u = n - first_down
                    pe.wait_ge(hid_lo_ready, i * 4 + (l * FT + 2 * u + 2))
                    last = isinstance(i, int) and u == N_DN - 1
                    order = [(kk, g) for g in range(KT) for kk in (0, 1)] if last else \
                        [(kk, g) for kk in (0, 1) for g in range(KT)]
                    for kk, g in order:
                        hk = bass.ds(i * 4 + (2 * u + kk), 1)
                        hh = [a[:, hk, :].rearrange("p u n -> p (u n)") for a in (hid_hi, hid_lo)]
                        cols = slice(kk * D + g * P, kk * D + (g + 1) * P)
                        ins = three(big[:, g // 2, (g % 2) * T:(g % 2 + 1) * T],
                                    (w_hi[:, n % SPLIT, cols], w_lo[:, n % SPLIT, cols]), hh,
                                    isinstance(i, int) and u == 0 and kk == 0 and g % 2 == 0,
                                    last and kk == 1)
                        if last and g % 2 and kk and g < KT - 1:
                            ins.then_inc(down_summed, 1)
                    ins.then_inc(w_used, 1)
                down_unit(0, first_down)
                stream(pe, first_down + 1, N_DN - 3, 2, down_unit)
                for n in range(first_down + N_DN - 2, first_down + N_DN):
                    down_unit(0, n)

            halves_at = lambda value, order: lambda n, a: feature_major(n, a, value, order, KT // 2)
            for u in range(N_EO):
                form = halves_at(MIX_AT[0], (4, 5, 6, 7, 0, 1, 2, 3)) if u == 0 else feature_major
                units(EO, EO + u, 1, form, x_updated, 0)
                if u >= 1:
                    norm_sum_of(1, 2 * u - 2, 2 * u)
            ffn(0, UP0, DN0, 1)
            mod_sum(2, ADA3, 16, aux[:, 1])
            norm_sum_of(2)
            mod_turn(2, 16, aux[:, 1])
            units(OI, OI, 12, feature_major, z_evicted, N_EI, h_from=NORM_AT[2])
            units(OI, OI + 12, 4, token_major, z_evicted, N_EI)
            pe.wait_ge(wrapped, 4)
            units(OI, OI + 16, 2, lambda n, a: token_major(n, a, staggered), z_evicted, N_EI)
            units(OI, OI + 18, 2, feature_major, z_evicted, N_EI)
            def dil_scores(bank, h, t):
                lane = slice((h % 2) * DH, (h % 2 + 1) * DH)

                def rows(first, g, tok0, tokens):
                    f = g * 4 + h // 2
                    return zo[lane, first + f // 2, (f % 2) * T + tok0:(f % 2) * T + tok0 + tokens]
                pe.matmul(bank[:, 0:T], rows(0, 0, t * P, P), rows(6, 0, 0, T), start=True, stop=True)
                for side in (0, 1):
                    tok0 = t * P + 64 * side
                    for block, g in enumerate((1, 2) if side == 0 else (2, 1)):
                        at0 = T + 64 * block
                        ins = pe.matmul(bank[64 * side:64 * side + 64, at0:at0 + 64], rows(0, g, tok0, 64),
                                        rows(6, g, tok0, 64), start=True, stop=True, skip_group_check=True)
                return ins

            def dil_values(dst, probs, h, t):
                for kt in range(TT):
                    v = zo[:, 12 + h // 4, kt * T + (h % 4) * DH:kt * T + (h % 4 + 1) * DH]
                    pe.matmul(dst, probs[:, kt * P:(kt + 1) * P], v, start=(kt == 0), stop=False, skip_group_check=True)
                for side in (0, 1):
                    v = zo[:, 14 + 2 * t + side, h * DH:(h + 1) * DH]
                    ins = pe.matmul(dst[64 * side:64 * side + 64, :], probs[:, T + 64 * side:T + 64 * side + 64], v,
                                    start=False, stop=True, skip_group_check=True)
                return ins

            def half_mods(s):
                if s == 2:
                    pe.wait_ge(z_evicted, N_EI + N_OI)
                    mod_sum(3, ADA3 + 16, 32, acc[:, 1], 0, 16)
                if s == 4:
                    pe.wait_ge(mod_kept, 4)

            attend(STEPS, ROW, dil_scores, dil_values, cpt, ctok, N_EI + N_OI, half_mods)

            pe.wait_ge(s_odd, 32)
            pe.wait_ge(pool_step, POOL_STEPS)
            for g in range(4):
                ins = pe.matmul(big[:, g // 2, (g % 2) * T:(g % 2 + 1) * T], poolw[:, g, :], pmean[:, g, :], start=True,
                                stop=True)
            ins.then_inc(pool_mixed, 1)
            mod_sum(3, ADAS, 32, acc[:, 1], 16, 32)

            for u in range(N_OO):
                form = halves_at(MIX_AT[1], range(KT)) if u == 0 else feature_major
                units(OO, OO + u, 1, form, x_updated, 16)
                if u == 0:
                    mod_turn(3, 32, big[:, 3])
                if u >= 1:
                    norm_sum_of(3, 2 * u - 2, 2 * u)
            ffn(1, UP1, DN1, 3)
            norm_sum_of(4)
            for k in range(KT):
                pe.wait_ge(y_ready, k + 1)
                for t in range(TT):
                    ins = pe.transpose(big[:, 2 * t + k // 4, (k % 4) * P:(k % 4 + 1) * P],
                                       work[:, k, t * P:(t + 1) * P], ident)
                if k % 4 == 3:
                    ins.then_inc(y_turned, 1)


_INS = ("x", "c", "ada_w", "ada_b", "norm_mix_g", "norm_ffn_g", "even_w_in", "even_w_out", "hgrn_lb_logits",
        "hgrn_norm_g", "na_rpb", "odd_w_in", "odd_w_out", "pool_w", "pool_scale", "ffn_w_up", "ffn_conv_w",
        "ffn_conv_b", "ffn_w_down", "final_norm_g")


def kernel(**inputs):
    import concourse.bacc as bacc
    from concourse.bass_utils import run_bass_kernel_spmd

    nc = bacc.Bacc("TRN2", target_bir_lowering=False, num_devices=1)
    arrays = {f"in_{name}": np.ascontiguousarray(inputs[name]) for name in _INS}
    arrays["in_shape_constants"] = shape_constants()
    args = [nc.dram_tensor(name, a.shape, mybir.dt.from_np(a.dtype), kind="ExternalInput").ap()
            for name, a in arrays.items()]
    out = nc.dram_tensor("out", (1, T, D), F32, kind="ExternalOutput").ap()
    encoder(nc, *args, out)
    r = run_bass_kernel_spmd(nc, [arrays], core_ids=[0])
    return r.results[0]["out"]
```
